# Optimizing a Trainium2 kernel written in Bass

```python
import math
import jax, jax.numpy as jnp
from jax import lax
import numpy as np

D_MODEL = 1024
BATCH = 1
SEQ = 256
DEPTH = 1

ATTN_HEAD_DIM = 64
ATTN_Q_HEADS = 16
ATTN_KV_HEADS = 2
ATTN_GROUP = ATTN_Q_HEADS // ATTN_KV_HEADS
ATTN_WIDTH = ATTN_Q_HEADS * ATTN_HEAD_DIM
ATTN_KV_WIDTH = ATTN_KV_HEADS * ATTN_HEAD_DIM
WINDOW = 128
ATTN_BLOCK = 128
HGRN_EXPAND = 128
HGRN_HEADS = D_MODEL // HGRN_EXPAND
HGRN_K = HGRN_EXPAND
HGRN_V = D_MODEL // HGRN_HEADS
HGRN_KEY_WIDTH = HGRN_HEADS * HGRN_K
HGRN_WIDTH = HGRN_HEADS * HGRN_V
CHUNK = 64
FFN_HIDDEN = -(-(8 * D_MODEL) // (3 * 256)) * 256
EPS = 1e-6
NEG_INF = -1e30
IN_SPLITS = (ATTN_WIDTH, ATTN_KV_WIDTH, ATTN_KV_WIDTH,
             HGRN_KEY_WIDTH, HGRN_KEY_WIDTH, HGRN_WIDTH, HGRN_WIDTH,
             D_MODEL, D_MODEL)
IN_WIDTH = sum(IN_SPLITS)


def rmsnorm(x, g):
    xf = x.astype(jnp.float32)
    y = xf * lax.rsqrt(jnp.mean(xf * xf, axis=-1, keepdims=True) + EPS)
    return (y * g.astype(jnp.float32)).astype(x.dtype)

def split_columns(p):
    idx = np.cumsum(np.array(IN_SPLITS))[:-1].tolist()
    return jnp.split(p, idx, axis=-1)

def sliding_window_sink_attention(q, k, v, sinks):
    B, S = q.shape[0], q.shape[1]
    nb = S // ATTN_BLOCK
    qb = q.reshape(B, nb, ATTN_BLOCK, ATTN_KV_HEADS, ATTN_GROUP, ATTN_HEAD_DIM)
    kb = k.reshape(B, nb, ATTN_BLOCK, ATTN_KV_HEADS, ATTN_HEAD_DIM)
    vb = v.reshape(B, nb, ATTN_BLOCK, ATTN_KV_HEADS, ATTN_HEAD_DIM)

    def with_prev(t):
        prev = jnp.concatenate([jnp.zeros_like(t[:, :1]), t[:, :-1]], axis=1)
        return jnp.concatenate([prev, t], axis=2)

    kw, vw = with_prev(kb), with_prev(vb)
    scale = 1.0 / math.sqrt(ATTN_HEAD_DIM)
    scores = jnp.einsum('bnqhgd,bnkhd->bnhgqk', qb, kw).astype(jnp.float32) * scale
    qi = jnp.arange(ATTN_BLOCK)[:, None]
    kj = jnp.arange(2 * ATTN_BLOCK)[None, :]
    rel = qi + ATTN_BLOCK - kj
    key_pos = jnp.arange(nb)[:, None, None] * ATTN_BLOCK - ATTN_BLOCK + kj[None]
    valid = (rel >= 0)[None] & (rel < WINDOW)[None] & (key_pos >= 0)
    scores = jnp.where(valid[None, :, None, None], scores, NEG_INF)
    sink = jnp.broadcast_to(
        sinks.astype(jnp.float32).reshape(1, 1, ATTN_KV_HEADS, ATTN_GROUP, 1, 1),
        scores.shape[:-1] + (1,))
    probs = jax.nn.softmax(jnp.concatenate([scores, sink], axis=-1), axis=-1)[..., :-1]
    out = jnp.einsum('bnhgqk,bnkhd->bnqhgd', probs.astype(v.dtype), vw)
    return out.reshape(B, S, ATTN_WIDTH)

def hgrn2_chunkwise(q, k, v, log_f):
    B, S, H, K = q.shape
    V = v.shape[-1]
    n = S // CHUNK

    def to_chunks(t):
        return t.reshape(B, n, CHUNK, H, t.shape[-1]).transpose(1, 0, 3, 2, 4)

    causal = jnp.tril(jnp.ones((CHUNK, CHUNK), dtype=bool))

    def step(state, inp):
        qc, kc, vc, gc = inp
        b = jnp.cumsum(gc, axis=2)
        b_mid = b[:, :, CHUNK // 2 - 1:CHUNK // 2]
        b_last = b[:, :, -1:]
        a = jnp.einsum('bhck,bhsk->bhcs', qc * jnp.exp(b - b_mid), kc * jnp.exp(b_mid - b))
        a = jnp.where(causal, a, 0.0)
        o = (jnp.einsum('bhcs,bhsv->bhcv', a, vc)
             + jnp.einsum('bhck,bhkv->bhcv', qc * jnp.exp(b), state))
        state = (jnp.exp(b_last)[:, :, 0, :, None] * state
                 + jnp.einsum('bhsk,bhsv->bhkv', kc * jnp.exp(b_last - b), vc))
        return state, o

    s0 = jnp.zeros((B, H, K, V), jnp.float32)
    _, o = lax.scan(step, s0, (to_chunks(q), to_chunks(k), to_chunks(v), to_chunks(log_f)))
    return o.transpose(1, 0, 3, 2, 4).reshape(B, S, H, V)

def hgrn2_branch(hq, hf, hi, hg, lb, norm_g):
    B, S = hq.shape[0], hq.shape[1]
    fp = hf.astype(jnp.float32)
    log_f = jnp.log(lb + (1.0 - lb) * jax.nn.sigmoid(fp))
    k = (1.0 - lb) * jax.nn.sigmoid(-fp)
    q = jax.nn.silu(hq.astype(jnp.float32))
    shp_k = (B, S, HGRN_HEADS, HGRN_K)
    o = hgrn2_chunkwise(q.reshape(shp_k), k.reshape(shp_k),
                        hi.astype(jnp.float32).reshape(B, S, HGRN_HEADS, HGRN_V),
                        log_f.reshape(shp_k))
    o = o * lax.rsqrt(jnp.mean(o * o, axis=-1, keepdims=True) + EPS)
    o = o.reshape(B, S, HGRN_WIDTH) * norm_g.astype(jnp.float32)
    o = o * jax.nn.sigmoid(hg.astype(jnp.float32))
    return o.astype(hq.dtype)

def first_inputs(seed: int = 0) -> dict:
    key = jax.random.key(seed)
    ks = jax.random.split(key, 20)
    D, F = D_MODEL, FFN_HIDDEN
    nrm = lambda k, shape, fan_in: jax.random.normal(k, shape, jnp.float32) * fan_in ** -0.5
    gain = lambda k, shape: 1.0 + 0.05 * jax.random.normal(k, shape, jnp.float32)
    return {
        "x": jax.random.normal(ks[0], (BATCH, SEQ, D), jnp.float32),
        "norm_mix_g": gain(ks[1], (DEPTH, D)),
        "w_in": nrm(ks[2], (DEPTH, D, IN_WIDTH), D),
        "b_in": 0.01 * jax.random.normal(ks[3], (DEPTH, IN_WIDTH), jnp.float32),
        "attn_sinks": 0.5 * jax.random.normal(ks[4], (DEPTH, ATTN_Q_HEADS), jnp.float32),
        "hgrn_lb_logits": gain(ks[5], (DEPTH + 1, HGRN_KEY_WIDTH)),
        "hgrn_norm_g": gain(ks[6], (DEPTH, HGRN_WIDTH)),
        "w_branch_attn": nrm(ks[7], (DEPTH, ATTN_WIDTH, D), ATTN_WIDTH),
        "w_branch_hgrn": nrm(ks[8], (DEPTH, HGRN_WIDTH, D), HGRN_WIDTH),
        "w_out": nrm(ks[9], (DEPTH, D, D), D),
        "norm_ffn_g": gain(ks[10], (DEPTH, D)),
        "w_ffn_gate": nrm(ks[11], (DEPTH, D, F), D),
        "w_ffn_up": nrm(ks[12], (DEPTH, D, F), D),
        "w_ffn_down": nrm(ks[13], (DEPTH, F, D), F),
        "norm_final_g": gain(ks[14], (D,)),
    }

def first_block(x, norm_mix_g, w_in, b_in, attn_sinks, hgrn_lb_logits, hgrn_norm_g,
              w_branch_attn, w_branch_hgrn, w_out, norm_ffn_g, w_ffn_gate, w_ffn_up,
              w_ffn_down, norm_final_g):
    lb_all = jnp.cumsum(jax.nn.softmax(hgrn_lb_logits.astype(jnp.float32), axis=0), axis=0)
    h = x
    for layer in range(DEPTH):
        u = rmsnorm(h, norm_mix_g[layer])
        p = jnp.einsum('bsd,de->bse', u, w_in[layer]) + b_in[layer]
        aq, ak, av, hq, hf, hi, hg, gate_a, gate_b = split_columns(p)
        y_attn = sliding_window_sink_attention(aq, ak, av, attn_sinks[layer])
        y_hgrn = hgrn2_branch(hq, hf, hi, hg, lb_all[layer], hgrn_norm_g[layer])
        ya = jnp.einsum('bse,ed->bsd', y_attn, w_branch_attn[layer])
        yb = jnp.einsum('bse,ed->bsd', y_hgrn, w_branch_hgrn[layer])
        merged = jax.nn.sigmoid(gate_a) * ya + jax.nn.sigmoid(gate_b) * yb
        h = h + jnp.einsum('bsd,de->bse', merged, w_out[layer])
        u = rmsnorm(h, norm_ffn_g[layer])
        z = (jax.nn.silu(jnp.einsum('bsd,df->bsf', u, w_ffn_gate[layer]))
             * jnp.einsum('bsd,df->bsf', u, w_ffn_up[layer]))
        h = h + jnp.einsum('bsf,fd->bsd', z, w_ffn_down[layer])
    return rmsnorm(h, norm_final_g)


D_MIX = D_MODEL
SSD_WIDTH = D_MIX // 2
ATTN_WIDTH_2 = D_MIX - SSD_WIDTH
SSD_HEAD_DIM = 64
SSD_HEADS = SSD_WIDTH // SSD_HEAD_DIM
SSD_GROUPS = 2
SSD_HPG = SSD_HEADS // SSD_GROUPS
SSD_STATE = 128
SSD_CONV = 4
SSD_CHUNK = CHUNK
XBC_DIM = SSD_WIDTH + 2 * SSD_GROUPS * SSD_STATE
ATTN_HEADS = ATTN_WIDTH_2 // ATTN_HEAD_DIM
LEFT_CHUNKS = 8
BAND = (LEFT_CHUNKS + 1) * CHUNK
MAX_REL = 128
N_REL = 2 * MAX_REL + 1
FFN_DIM = 2816
FFN_CONV = 3
ADA_DIM = 6 * D_MODEL
IN_SIZES = (SSD_WIDTH, XBC_DIM, SSD_HEADS, ATTN_WIDTH_2, ATTN_WIDTH_2, ATTN_WIDTH_2)
IN_DIM = sum(IN_SIZES)
IN_SPLITS_2 = [int(v) for v in np.cumsum(IN_SIZES)[:-1]]


def rmsnorm_2(x, w):
    xf = x.astype(jnp.float32)
    y = xf * lax.rsqrt(jnp.mean(xf * xf, axis=-1, keepdims=True) + EPS)
    return (y * w.astype(jnp.float32)).astype(x.dtype)

def causal_dwconv(x, w):
    k, ch = w.shape
    return lax.conv_general_dilated(x, w[:, None, :].astype(x.dtype), window_strides=(1,),
                                    padding=[(k - 1, 0)], dimension_numbers=('NWC', 'WIO', 'NWC'),
                                    feature_group_count=ch)

def ssd_scan(xdt, adt, bm, cm):
    b, s = xdt.shape[:2]
    nc = s // SSD_CHUNK
    L = SSD_CHUNK
    X = xdt.reshape(b, nc, L, SSD_GROUPS, SSD_HPG, SSD_HEAD_DIM)
    A = adt.reshape(b, nc, L, SSD_GROUPS, SSD_HPG)
    Bm = bm.reshape(b, nc, L, SSD_GROUPS, SSD_STATE)
    Cm = cm.reshape(b, nc, L, SSD_GROUPS, SSD_STATE)
    a_cs = jnp.cumsum(A, axis=2)
    seg = a_cs[:, :, :, None] - a_cs[:, :, None]
    causal = jnp.tril(jnp.ones((L, L), dtype=bool))[:, :, None, None]
    decay_ls = jnp.exp(jnp.where(causal, seg, -jnp.inf))
    cb = jnp.einsum('bclgn,bcsgn->bclsg', Cm, Bm)
    y_diag = jnp.einsum('bclsg,bclsge,bcsgep->bclgep', cb, decay_ls, X)
    decay_to_end = jnp.exp(a_cs[:, :, -1:] - a_cs)
    states = jnp.einsum('bclgn,bclge,bclgep->bcgepn', Bm, decay_to_end, X)
    chunk_decay = jnp.exp(a_cs[:, :, -1])

    def step(h, inp):
        st, dec = inp
        return h * dec[..., None, None] + st, h

    _, prev = lax.scan(step, jnp.zeros_like(states[:, 0]),
                       (jnp.moveaxis(states, 1, 0), jnp.moveaxis(chunk_decay, 1, 0)))
    prev = jnp.moveaxis(prev, 0, 1)
    y_off = jnp.einsum('bclgn,bcgepn,bclge->bclgep', Cm, prev, jnp.exp(a_cs))
    return (y_diag + y_off).reshape(b, s, SSD_HEADS, SSD_HEAD_DIM)

def ssd_mixer(z, xbc, dt_raw, conv_w, conv_b, dt_bias, a_log, d_skip, norm_w):
    b, s, _ = xbc.shape
    xbc = jax.nn.silu(causal_dwconv(xbc, conv_w) + conv_b.astype(xbc.dtype))
    xs, bm, cm = jnp.split(xbc.astype(jnp.float32), [SSD_WIDTH, SSD_WIDTH + SSD_GROUPS * SSD_STATE], axis=-1)
    xs = xs.reshape(b, s, SSD_HEADS, SSD_HEAD_DIM)
    bm = bm.reshape(b, s, SSD_GROUPS, SSD_STATE)
    cm = cm.reshape(b, s, SSD_GROUPS, SSD_STATE)
    dt = jax.nn.softplus(dt_raw.astype(jnp.float32) + dt_bias.astype(jnp.float32))
    A = -jnp.exp(a_log.astype(jnp.float32))
    y = ssd_scan(xs * dt[..., None], dt * A, bm, cm)
    y = y + d_skip.astype(jnp.float32)[:, None] * xs
    y = y.reshape(b, s, SSD_WIDTH) * jax.nn.silu(z.astype(jnp.float32))
    return rmsnorm_2(y, norm_w).astype(z.dtype)

def chunk_attention(q, k, v, rel_bias):
    b, s, _ = q.shape
    nc = s // CHUNK
    pad = LEFT_CHUNKS * CHUNK
    qc = q.reshape(b, nc, CHUNK, ATTN_HEADS, ATTN_HEAD_DIM)

    def band(t):
        tp = jnp.pad(t.reshape(b, s, ATTN_HEADS, ATTN_HEAD_DIM), ((0, 0), (pad, 0), (0, 0), (0, 0)))
        tp = tp.reshape(b, nc + LEFT_CHUNKS, CHUNK, ATTN_HEADS, ATTN_HEAD_DIM)
        return jnp.concatenate([tp[:, w:w + nc] for w in range(LEFT_CHUNKS + 1)], axis=2)

    kb, vb = band(k), band(v)
    scores = jnp.einsum('bcqhd,bckhd->bhcqk', qc, kb).astype(jnp.float32) * (ATTN_HEAD_DIM ** -0.5)
    qi = jnp.arange(CHUNK)[:, None]
    kj = jnp.arange(BAND)[None, :]
    rel_idx = jnp.clip(qi - kj + pad, -MAX_REL, MAX_REL) + MAX_REL
    bias = rel_bias.astype(jnp.float32)[:, rel_idx]
    key_pos = jnp.arange(nc)[:, None] * CHUNK - pad + kj
    valid = (key_pos >= 0)[:, None, :]
    scores = jnp.where(valid, scores + bias[:, None], jnp.finfo(jnp.float32).min)
    p = jax.nn.softmax(scores, axis=-1).astype(v.dtype)
    o = jnp.einsum('bhcqk,bckhd->bcqhd', p, vb)
    return o.reshape(b, s, ATTN_WIDTH_2)

def conv_ffn(h, w_up, conv_w, w_down):
    u = causal_dwconv(h @ w_up, conv_w)
    g, val = jnp.split(u, 2, axis=-1)
    return (jax.nn.silu(g) * val) @ w_down

def second_inputs(seed: int = 0) -> dict:
    key = jax.random.key(seed)
    ks = jax.random.split(key, 24)
    f32 = jnp.float32
    nrm = lambda k, shape, sc: jax.random.normal(k, shape, f32) * sc
    u = jax.random.uniform(ks[10], (DEPTH, SSD_HEADS), f32)
    dt0 = jnp.exp(u * (jnp.log(0.1) - jnp.log(0.001)) + jnp.log(0.001))
    return {
        "x": nrm(ks[0], (BATCH, SEQ, D_MODEL), 1.0),
        "c": nrm(ks[1], (BATCH, D_MODEL), 1.0),
        "norm_mix_w": 1.0 + nrm(ks[2], (DEPTH, D_MODEL), 0.05),
        "w_ada": nrm(ks[3], (DEPTH, D_MODEL, ADA_DIM), 0.02),
        "b_ada": nrm(ks[4], (DEPTH, ADA_DIM), 0.02),
        "w_in": nrm(ks[5], (DEPTH, D_MODEL, IN_DIM), D_MODEL ** -0.5),
        "ssd_conv_w": nrm(ks[6], (DEPTH, SSD_CONV, XBC_DIM), SSD_CONV ** -0.5),
        "ssd_conv_b": nrm(ks[7], (DEPTH, XBC_DIM), 0.02),
        "dt_bias": dt0 + jnp.log(-jnp.expm1(-dt0)),
        "a_log": jnp.log(jax.random.uniform(ks[8], (DEPTH, SSD_HEADS), f32, 1.0, 16.0)),
        "d_skip": 1.0 + nrm(ks[9], (DEPTH, SSD_HEADS), 0.1),
        "ssd_norm_w": 1.0 + nrm(ks[11], (DEPTH, SSD_WIDTH), 0.05),
        "rel_bias": nrm(ks[12], (DEPTH, ATTN_HEADS, N_REL), 0.5),
        "w_out": nrm(ks[13], (DEPTH, D_MIX, D_MODEL), D_MIX ** -0.5),
        "norm_ffn_w": 1.0 + nrm(ks[14], (DEPTH, D_MODEL), 0.05),
        "w_up": nrm(ks[15], (DEPTH, D_MODEL, 2 * FFN_DIM), D_MODEL ** -0.5),
        "ffn_conv_w": nrm(ks[16], (DEPTH, FFN_CONV, 2 * FFN_DIM), FFN_CONV ** -0.5),
        "w_down": nrm(ks[17], (DEPTH, FFN_DIM, D_MODEL), FFN_DIM ** -0.5),
        "final_norm_w": 1.0 + nrm(ks[18], (D_MODEL,), 0.05),
    }

def second_block(x, c, norm_mix_w, w_ada, b_ada, w_in, ssd_conv_w, ssd_conv_b, dt_bias, a_log, d_skip,
              ssd_norm_w, rel_bias, w_out, norm_ffn_w, w_up, ffn_conv_w, w_down, final_norm_w):
    c_act = jax.nn.silu(c)
    for l in range(DEPTH):
        mod = (c_act @ w_ada[l] + b_ada[l])[:, None, :]
        sh_m, sc_m, g_m, sh_f, sc_f, g_f = jnp.split(mod, 6, axis=-1)
        h = rmsnorm_2(x, norm_mix_w[l]) * (1 + sc_m) + sh_m
        z, xbc, dt_raw, q, k, v = jnp.split(h @ w_in[l], IN_SPLITS_2, axis=-1)
        y_ssd = ssd_mixer(z, xbc, dt_raw, ssd_conv_w[l], ssd_conv_b[l], dt_bias[l], a_log[l],
                          d_skip[l], ssd_norm_w[l])
        y_att = chunk_attention(q, k, v, rel_bias[l])
        x = x + g_m * (jnp.concatenate([y_ssd, y_att], axis=-1) @ w_out[l])
        h = rmsnorm_2(x, norm_ffn_w[l]) * (1 + sc_f) + sh_f
        x = x + g_f * conv_ffn(h, w_up[l], ffn_conv_w[l], w_down[l])
    return rmsnorm_2(x, final_norm_w)


def setup_inputs(seed=0):
    out = dict(first_inputs(seed))
    for name, value in second_inputs(seed + 1).items():
        if name != "x":
            out[name + "_2"] = value
    return out


def reference(
    x, norm_mix_g, w_in, b_in, attn_sinks, hgrn_lb_logits, hgrn_norm_g, w_branch_attn,
    w_branch_hgrn, w_out, norm_ffn_g, w_ffn_gate, w_ffn_up, w_ffn_down, norm_final_g, c_2,
    norm_mix_w_2, w_ada_2, b_ada_2, w_in_2, ssd_conv_w_2, ssd_conv_b_2, dt_bias_2, a_log_2,
    d_skip_2, ssd_norm_w_2, rel_bias_2, w_out_2, norm_ffn_w_2, w_up_2, ffn_conv_w_2, w_down_2,
    final_norm_w_2,
):
    x = first_block(
        x, norm_mix_g, w_in, b_in, attn_sinks, hgrn_lb_logits, hgrn_norm_g, w_branch_attn,
        w_branch_hgrn, w_out, norm_ffn_g, w_ffn_gate, w_ffn_up, w_ffn_down, norm_final_g,
    )
    return second_block(
        x, c_2, norm_mix_w_2, w_ada_2, b_ada_2, w_in_2, ssd_conv_w_2, ssd_conv_b_2, dt_bias_2,
        a_log_2, d_skip_2, ssd_norm_w_2, rel_bias_2, w_out_2, norm_ffn_w_2, w_up_2,
        ffn_conv_w_2, w_down_2, final_norm_w_2,
    )


_drawn_inputs = setup_inputs


def setup_inputs(seed=0):
    import zlib

    import numpy as np

    out = dict(_drawn_inputs(seed))
    spreads = {}
    factors = {'b_in': 5.032,
     'attn_sinks': 8.0,
     'hgrn_lb_logits': 8.0,
     'hgrn_norm_g': 3.268,
     'norm_mix_w_2': 2.731,
     'ssd_conv_b_2': 8.0,
     'ssd_norm_w_2': 3.632,
     'norm_ffn_w_2': 3.052,
     'd_skip_2': 21.665}
    for name, (base, spread) in spreads.items():
        noise = np.random.default_rng([zlib.crc32(name.encode()), seed]).standard_normal(out[name].shape)
        drawn = base * np.exp(spread * noise) if base else spread * noise
        out[name] = __import__('jax').numpy.asarray(drawn.astype(out[name].dtype))
    for name, factor in factors.items():
        out[name] = (out[name] * factor).astype(out[name].dtype)
    return out
```

```python
from contextlib import ExitStack

import concourse.bass as bass
from concourse import mybir

F32 = mybir.dt.float32
F32R = mybir.dt.float32r
BF16 = mybir.dt.bfloat16
U32 = mybir.dt.uint32
ACT = mybir.ActivationFunctionType
ALU = mybir.AluOpType
AX_X = mybir.AxisListType.X

P = 128
D = 1024
KD = D // P
T = 256
TB = T // P
DH = 64
C = 64
FF = 2816
KF = FF // P
EPS = 1e-6
NEG = -1e30
NRAW, NHL = 4, 3
AHEAD = NHL - 1
KP = 4
W = 512

PAR = {}
NPAR = 0
for _name, _n in (("norm_mix_g", 8), ("b_in", 58), ("lb0", 8), ("lb1", 8), ("hgrn_norm_g", 8),
                  ("norm_ffn_g", 8), ("norm_final_g", 8), ("c", 8), ("norm_mix_w_2", 8), ("b_ada", 48),
                  ("conv_w", 32), ("conv_b", 8), ("d_skip", 4), ("ssd_norm_w", 4), ("norm_ffn_w_2", 8),
                  ("ffn_conv_w", 132), ("final_norm_w", 8), ("sinks", 16), ("dt_bias", 8), ("a_log", 8)):
    PAR[_name] = (NPAR, _n)
    NPAR += _n


def cm_tiles(n=4):
    return [("cm", m, m * P) for m in range(n)]


def tm_tiles(off, width):
    return [("tm", 2 + j, off, width, j) for j in range(TB)]


def group(weights, segments, tiles, evac, operand, kblocks=KD, kbase=0):
    parts = [(k, min(KP, kblocks - k)) for k in range(0, kblocks, KP)]
    return dict(w=weights, seg=segments, tiles=tiles, evac=evac, act=operand, parts=parts, kbase=kbase)


GROUPS = {}
for _i in range(2):
    for _name, _c in (("q", 0), ("hq", 1280), ("hf", 2304), ("hg", 4352), ("ga", 5376), ("gb", 6400)):
        GROUPS[f"{_name}{_i}"] = group("w_in", [(_c + _i * W, W)], cm_tiles(), "AAAA", "P1")
    GROUPS[f"hi{_i}"] = group("w_in", [(3328 + _i * W, W)], tm_tiles(0, W), "DD", "P1")
    GROUPS[f"ba{_i}"] = group("w_branch_attn", [(_i * W, W)], cm_tiles(), "DDDD", "PY")
    GROUPS[f"bh{_i}"] = group("w_branch_hgrn", [(_i * W, W)], cm_tiles(), "DDDD", "PY")
    GROUPS[f"out{_i}"] = group("w_out", [(_i * W, W)], cm_tiles(), "DDDD", "P1")
    GROUPS[f"down{_i}"] = group("w_ffn_down", [(_i * W, W)], cm_tiles(), "DDDD", "Z", KF)
    GROUPS[f"oo{_i}"] = group("w_out_2", [(_i * W, W)], cm_tiles(), "DDDD", "PY")
    GROUPS[f"dd{_i}"] = group("w_down_2", [(_i * W, W)], cm_tiles(), "DDDD", "Z", KF)
GROUPS["kv"] = group("w_in", [(1024, 256)], [("cm", 0, 0)] + tm_tiles(128, 128), "ADD", "P1")
NF = FF // 256
for _i in range(NF):
    GROUPS[f"f{_i}"] = group(("w_ffn_gate", "w_ffn_up"), [(_i * 256, 256), (_i * 256, 256)], cm_tiles(), "AADD", "P1")
    GROUPS[f"u{_i}"] = group("w_up_2", [(_i * 256, 256), (FF + _i * 256, 256)], cm_tiles(), "AAAA", "P1")
for _name, _c in (("z", 0), ("xs", 512), ("bc", 1024), ("q2", 1544), ("k2", 2056)):
    GROUPS[_name] = group("w_in_2", [(_c, W)], cm_tiles(), "AAAA", "P1")
GROUPS["v2"] = group("w_in_2", [(2568, W)], tm_tiles(0, W), "DD", "P1")

UNITS = [(1, 0, 0, 8, 1), (1, 0, 8, 8, 1), (1, 1, 0, 4, 2), (1, 1, 4, 4, 2), (1, 1, 8, 4, 2), (1, 1, 12, 4, 2),
         (2, 0, 0, 8, 1), (2, 1, 0, 4, 2), (2, 1, 4, 4, 2)]
NU1 = 6


WITH_ADA = [(_n, _i) for _n in ("q0", "q1", "bh0", "bh1", "out0") for _i in range(2)] + [("out1", 0)]
WITH_ADA += [(f"f{_i}", 0) for _i in range(NF)] + [("down0", 0), ("down0", 1)]


class Signals:
    pass


def timeline():
    tl = [("load_x",), ("norm", 0)]
    ada = iter(range(24))

    def gemm(name, *after):
        parts = len(GROUPS[name]["parts"])
        for i in range(parts):
            tl.append(("panel", name, i))
            if (name, i) in WITH_ADA:
                j = next(ada)
                tl.append(("ada", j))
                if j % 2:
                    tl.append(("ada_sum", j // 2))
            if i == parts - 1:
                tl.append(("evac", name))
            if i < len(after):
                tl.extend(after[i])

    def X(u):
        return [("pv", u - 1)] * (u > 0) + [("scores", u)] * (u < NU1)

    def Y(u):
        return [("pt", u)] * (u < NU1) + [("yT", u - 1)] * (u > 0)

    gemm("q0", [], [("setup",)])
    gemm("q1")
    gemm("kv", [], X(0))
    gemm("ga0", Y(0), X(1))
    gemm("ga1", Y(1), X(2))
    gemm("hq0", Y(2), X(3))
    gemm("hf0", Y(3), X(4))
    gemm("hi0", Y(4), X(5) + [("hprep", 0, 0)])
    gemm("hg0", Y(5) + [("hprep", 0, 1)], X(6) + [("hprep", 0, 2)])
    gemm("gb0", Y(6) + [("hprep", 0, 3)], [])
    gemm("gb1", [("hA", 0)], [("hB", 0)])
    gemm("hq1", [("hC", 0), ("hD", 0)])
    gemm("hf1", [], [("hprep", 1, 0)])
    gemm("hi1", [("hprep", 1, 1)], [("hprep", 1, 2)])
    gemm("hg1", [("hprep", 1, 3)])
    gemm("ba0", [("hA", 1)], [("hB", 1)])
    gemm("ba1", [("hC", 1)], [("hsplit", 0), ("hD", 1), ("hsplit", 1)])
    gemm("bh0")
    gemm("bh1", [], [("merge",)])
    gemm("out0")
    gemm("out1", [], [("norm", 1)])
    for i in range(NF):
        gemm(f"f{i}")
    gemm("down0")
    gemm("down1", [("mod",)], [], [], [], [], [("norm", 2)])
    assert next(ada, None) is None, "every panel of w_ada has its place"
    gemm("xs")
    gemm("bc", [("dt",)])
    gemm("q2", [], [("xdt",), ("sA", 0)])
    gemm("k2", [("sY", 0), ("sA", 1)], [("sY", 1), ("scores", 6)])
    gemm("v2", [("pt", 6)], [("pv", 6), ("scores", 7)])
    gemm("z", [("pt", 7), ("yT", 6)], [("pv", 7), ("scores", 8), ("snorm",)])
    gemm("oo0", [("pt", 8), ("yT", 7), ("pv", 8), ("yT", 8)])
    gemm("oo1", [], [("norm", 3)])
    for i in range(NF):
        gemm(f"u{i}")
    gemm("dd0")
    gemm("dd1", [], [], [], [], [], [("norm", 4), ("store",)])
    return tl


def build(nc, IN, out):
    TL = timeline()
    panels = [(e[1], e[2]) for e in TL if e[0] == "panel"]
    PIDX = {p: i for i, p in enumerate(panels)}

    stream = [("w", q) for q in range(AHEAD)]
    for e in TL:
        if e[0] == "panel" and PIDX[e[1:]] + AHEAD < len(panels):
            stream.append(("w", PIDX[e[1:]] + AHEAD))
        elif e[0] == "ada":
            stream.append(("ada", e[1]))
    SIDX = {s: i for i, s in enumerate(stream)}
    slot_loads, landed = [0] * NRAW, []
    for i, (kind, q) in enumerate(stream):
        slot_loads[i % NRAW] += 16 * (len(GROUPS[panels[q][0]]["seg"]) if kind == "w" else 1)
        landed.append(slot_loads[i % NRAW])

    with ExitStack() as ctx:
        on = Signals()
        on.a_exp = ctx.enter_context(nc.semaphore("a_exp"))
        on.abc_psum = ctx.enter_context(nc.semaphore("abc_psum"))
        on.ada_done = ctx.enter_context(nc.semaphore("ada_done"))
        on.ada_psum = ctx.enter_context(nc.semaphore("ada_psum"))
        on.adt = ctx.enter_context(nc.semaphore("adt"))
        on.bcast = ctx.enter_context(nc.semaphore("bcast"))
        on.bm_psum = ctx.enter_context(nc.semaphore("bm_psum"))
        on.cb = ctx.enter_context(nc.semaphore("cb"))
        on.cb_psum = ctx.enter_context(nc.semaphore("cb_psum"))
        on.consts = ctx.enter_context(nc.semaphore("consts"))
        on.conv0 = ctx.enter_context(nc.semaphore("conv0"))
        on.conv_done = ctx.enter_context(nc.semaphore("conv_done"))
        on.dsink = ctx.enter_context(nc.semaphore("dsink"))
        on.dt_abs = ctx.enter_context(nc.semaphore("dt_abs"))
        on.dt_e = ctx.enter_context(nc.semaphore("dt_e"))
        on.dt_ln = ctx.enter_context(nc.semaphore("dt_ln"))
        on.dt_psum = ctx.enter_context(nc.semaphore("dt_psum"))
        on.dtw_hi = ctx.enter_context(nc.semaphore("dtw_hi"))
        on.dtw_lo = ctx.enter_context(nc.semaphore("dtw_lo"))
        on.dve_step = ctx.enter_context(nc.semaphore("dve_step"))
        on.esink = ctx.enter_context(nc.semaphore("esink"))
        on.evac_act = ctx.enter_context(nc.semaphore("evac_act"))
        on.evac_dve = ctx.enter_context(nc.semaphore("evac_dve"))
        on.ext_done = ctx.enter_context(nc.semaphore("ext_done"))
        on.ext_out = ctx.enter_context(nc.semaphore("ext_out"))
        on.g_done = ctx.enter_context(nc.semaphore("g_done"))
        on.hE1 = ctx.enter_context(nc.semaphore("hE1"))
        on.hE2 = ctx.enter_context(nc.semaphore("hE2"))
        on.hE3 = ctx.enter_context(nc.semaphore("hE3"))
        on.hE4 = ctx.enter_context(nc.semaphore("hE4"))
        on.hE5 = ctx.enter_context(nc.semaphore("hE5"))
        on.hKk = ctx.enter_context(nc.semaphore("hKk"))
        on.hKp = ctx.enter_context(nc.semaphore("hKp"))
        on.hQp = ctx.enter_context(nc.semaphore("hQp"))
        on.hQq = ctx.enter_context(nc.semaphore("hQq"))
        on.hS = ctx.enter_context(nc.semaphore("hS"))
        on.h_final = ctx.enter_context(nc.semaphore("h_final"))
        on.hat = ctx.enter_context(nc.semaphore("hat"))
        on.hat_psum = ctx.enter_context(nc.semaphore("hat_psum"))
        on.hb_done = ctx.enter_context(nc.semaphore("hb_done"))
        on.hdl = ctx.enter_context(nc.semaphore("hdl"))
        on.hdm = ctx.enter_context(nc.semaphore("hdm"))
        on.hf_log = ctx.enter_context(nc.semaphore("hf_log"))
        on.hfin = ctx.enter_context(nc.semaphore("hfin"))
        on.hk_done = ctx.enter_context(nc.semaphore("hk_done"))
        on.hkt = ctx.enter_context(nc.semaphore("hkt"))
        on.hkt_psum = ctx.enter_context(nc.semaphore("hkt_psum"))
        on.hkv_psum = ctx.enter_context(nc.semaphore("hkv_psum"))
        on.hq_done = ctx.enter_context(nc.semaphore("hq_done"))
        on.hs_done = ctx.enter_context(nc.semaphore("hs_done"))
        on.hsh = ctx.enter_context(nc.semaphore("hsh"))
        on.in_R2 = ctx.enter_context(nc.semaphore("in_R2"))
        on.in_brow = ctx.enter_context(nc.semaphore("in_brow"))
        on.in_dtw = ctx.enter_context(nc.semaphore("in_dtw"))
        on.in_par = ctx.enter_context(nc.semaphore("in_par"))
        on.in_rel = ctx.enter_context(nc.semaphore("in_rel"))
        on.in_x = [ctx.enter_context(nc.semaphore(f"in_x{b}")) for b in range(4)]
        on.k2_half = ctx.enter_context(nc.semaphore("k2_half"))
        on.kz = ctx.enter_context(nc.semaphore("kz"))
        on.kz_zero = ctx.enter_context(nc.semaphore("kz_zero"))
        on.lb_diff = ctx.enter_context(nc.semaphore("lb_diff"))
        on.lb_sig = ctx.enter_context(nc.semaphore("lb_sig"))
        on.c_silu = ctx.enter_context(nc.semaphore("c_silu"))
        on.merged = ctx.enter_context(nc.semaphore("merged"))
        on.mh = ctx.enter_context(nc.semaphore("mh"))
        on.mixed = ctx.enter_context(nc.semaphore("mixed"))
        on.negb = ctx.enter_context(nc.semaphore("negb"))
        on.negmax = ctx.enter_context(nc.semaphore("negmax"))
        on.o_bcast = ctx.enter_context(nc.semaphore("o_bcast"))
        on.o_copy = ctx.enter_context(nc.semaphore("o_copy"))
        on.o_psum = ctx.enter_context(nc.semaphore("o_psum"))
        on.o_rt = ctx.enter_context(nc.semaphore("o_rt"))
        on.o_rd = ctx.enter_context(nc.semaphore("o_rd"))
        on.o_sq = ctx.enter_context(nc.semaphore("o_sq"))
        on.oss_psum = ctx.enter_context(nc.semaphore("oss_psum"))
        on.ot_done = ctx.enter_context(nc.semaphore("ot_done"))
        on.ot_psum = ctx.enter_context(nc.semaphore("ot_psum"))
        on.out_done = ctx.enter_context(nc.semaphore("out_done"))
        on.out_part = ctx.enter_context(nc.semaphore("out_part"))
        on.panel_done = ctx.enter_context(nc.semaphore("panel_done"))
        on.pool_step = ctx.enter_context(nc.semaphore("pool_step"))
        on.probs = ctx.enter_context(nc.semaphore("probs"))
        on.probs_part = ctx.enter_context(nc.semaphore("probs_part"))
        on.pt_done = ctx.enter_context(nc.semaphore("pt_done"))
        on.pt_part = ctx.enter_context(nc.semaphore("pt_part"))
        on.pt_psum = ctx.enter_context(nc.semaphore("pt_psum"))
        on.pv_done = ctx.enter_context(nc.semaphore("pv_done"))
        on.pv_psum = ctx.enter_context(nc.semaphore("pv_psum"))
        on.act_fetch = ctx.enter_context(nc.semaphore("act_fetch"))
        on.hg_done = ctx.enter_context(nc.semaphore("hg_done"))
        on.sq2_done = ctx.enter_context(nc.semaphore("sq2_done"))
        on.ms2_done = ctx.enter_context(nc.semaphore("ms2_done"))
        on.rt2_done = ctx.enter_context(nc.semaphore("rt2_done"))
        on.rd2_done = ctx.enter_context(nc.semaphore("rd2_done"))
        on.rt_done = ctx.enter_context(nc.semaphore("rt_done"))
        on.rd_done = ctx.enter_context(nc.semaphore("rd_done"))
        on.scores_done = ctx.enter_context(nc.semaphore("scores_done"))
        on.seg = ctx.enter_context(nc.semaphore("seg"))
        on.seg_exp = ctx.enter_context(nc.semaphore("seg_exp"))
        on.sig_part = ctx.enter_context(nc.semaphore("sig_part"))
        on.snh = ctx.enter_context(nc.semaphore("snh"))
        on.snorm_done = ctx.enter_context(nc.semaphore("snorm_done"))
        on.sq_done = ctx.enter_context(nc.semaphore("sq_done"))
        on.ss_done = ctx.enter_context(nc.semaphore("ss_done"))
        on.stored = ctx.enter_context(nc.semaphore("stored"))
        on.sy = ctx.enter_context(nc.semaphore("sy"))
        on.sy_psum = ctx.enter_context(nc.semaphore("sy_psum"))
        on.tile_done = ctx.enter_context(nc.semaphore("tile_done"))
        on.tmp_done = ctx.enter_context(nc.semaphore("tmp_done"))
        on.u_ready = ctx.enter_context(nc.semaphore("u_ready"))
        on.u_silu = ctx.enter_context(nc.semaphore("u_silu"))
        on.uconv0 = ctx.enter_context(nc.semaphore("uconv0"))
        on.uconv_done = ctx.enter_context(nc.semaphore("uconv_done"))
        on.uh_done = ctx.enter_context(nc.semaphore("uh_done"))
        on.ur_zero = ctx.enter_context(nc.semaphore("ur_zero"))
        on.w_hi = ctx.enter_context(nc.semaphore("w_hi"))
        on.w_lo = ctx.enter_context(nc.semaphore("w_lo"))
        on.x_done = ctx.enter_context(nc.semaphore("x_done"))
        on.x_psum = ctx.enter_context(nc.semaphore("x_psum"))
        on.xc_done = ctx.enter_context(nc.semaphore("xc_done"))
        on.xd = ctx.enter_context(nc.semaphore("xd"))
        on.xd_psum = ctx.enter_context(nc.semaphore("xd_psum"))
        on.xr_zero = ctx.enter_context(nc.semaphore("xr_zero"))
        on.yT_done = ctx.enter_context(nc.semaphore("yT_done"))
        on.yT_psum = ctx.enter_context(nc.semaphore("yT_psum"))
        on.yTh = ctx.enter_context(nc.semaphore("yTh"))
        on.yrt = ctx.enter_context(nc.semaphore("yrt"))
        on.yrd = ctx.enter_context(nc.semaphore("yrd"))
        on.ybcast = ctx.enter_context(nc.semaphore("ybcast"))
        on.ysq = ctx.enter_context(nc.semaphore("ysq"))
        on.yss = ctx.enter_context(nc.semaphore("yss"))
        on.ytmp = ctx.enter_context(nc.semaphore("ytmp"))
        on.yz = ctx.enter_context(nc.semaphore("yz"))
        on.z_silu = ctx.enter_context(nc.semaphore("z_silu"))
        on.z_ready = ctx.enter_context(nc.semaphore("z_ready"))
        on.zh_done = ctx.enter_context(nc.semaphore("zh_done"))
        on.zt_done = ctx.enter_context(nc.semaphore("zt_done"))
        on.raw = [ctx.enter_context(nc.semaphore(f"raw{i}")) for i in range(NRAW)]

        TILE, USED, EV = {}, {}, {}
        tiles = plain = 0
        ev = {"A": 0, "D": 0}
        for name, part in panels:
            g = GROUPS[name]
            if part == len(g["parts"]) - 1:
                for m in range(len(g["tiles"])):
                    tiles += 1
                    TILE[name, m] = tiles
                    ev[g["evac"][m]] += 1
                    EV[name, m] = (on.evac_act if g["evac"][m] == "A" else on.evac_dve, ev[g["evac"][m]])
                USED[PIDX[name, part]] = (on.tile_done, tiles)
            else:
                plain += 1
                USED[PIDX[name, part]] = (on.panel_done, plain)
        BANKFREE, last = {}, {}
        for name, part in panels:
            if part == 0:
                for m, t in enumerate(GROUPS[name]["tiles"]):
                    if t[1] in last:
                        BANKFREE[name, m] = last[t[1]]
                for m, t in enumerate(GROUPS[name]["tiles"]):
                    last[t[1]] = EV[name, m]

        def sb(name, shape, dt=F32):
            return ctx.enter_context(nc.sbuf_tensor(name, shape, dt))

        raw = sb("raw", [P, NRAW, KP, W])
        wH = sb("wH", [P, NHL, KP, W], F32R)
        wL = sb("wL", [P, NHL, KP, W], F32R)
        p1H = sb("p1H", [P, KD, T], F32R)
        p1L = sb("p1L", [P, KD, T], F32R)
        hT = sb("hT", [P, KD, T])
        SCRK = 70
        arena = sb("arena", [P, (16 + SCRK) * 256])
        base = nc.sbuf_base - (16 + SCRK) * 1024

        def at(name, kb, shape, dt):
            return nc.alloc_sbuf_tensor_at(name, shape, dt, offset=base + kb * 1024)

        pyH = at("pyH", 0, [P, KD, T], F32R)
        pyL = at("pyL", 8, [P, KD, T], F32R)
        zH = at("zH", 0, [P, KF, T], F32R)
        zL = at("zL", 22, [P, KF, T], F32R)

        def scr(kb, *dims):
            n = 1
            for d in dims:
                n *= d
            v = arena[:, int((16 + kb) * 256):int((16 + kb) * 256) + n]
            if len(dims) == 1:
                return v
            names = "abc"[:len(dims)]
            return v.rearrange(f"p ({' '.join(names)}) -> p {' '.join(names)}", **dict(zip(names[1:], dims[1:])))

        xtok = scr(12, TB, D)
        vrow, dtw, ext = scr(10, P), scr(10.5, KD, 8), scr(40, 384)[0:8]
        SQ, TMP, SQ2, HG = scr(44, KD, T), scr(52, KD, T), scr(28, KD, T), scr(36, KD, T)
        aQ, aK, aKZ, aV = scr(0, KD, T), scr(8, T), scr(66, 4, T), scr(9, TB, P)
        PR, PT, YT = scr(12, 8, P), scr(16, 8, P), scr(20, 512)
        hQp, hKp, hAT, hKT, hS = scr(0, 4, T), scr(4, 4, T), scr(8, 8, P), scr(12, TB, 512), scr(16, 3, 512)
        GA, GB = scr(22, KD, T), scr(30, KD, T)
        hQ, hK, hB, T1, T2 = scr(38, 4, T), scr(42, 4, T), scr(46, 4, T), scr(50, 4, T), scr(54, 4, T)
        hV, hG = scr(58, TB, 512), scr(62, 4, T)
        YF0 = scr(66, 4, T)
        XC, XR = scr(0, 8, T), scr(8, 4, T + 3)
        SG, CB, XD = scr(22, 4, 384), scr(28, 384), scr(30, TB, 512)
        sY, sZ, sT = scr(34, 4, T), scr(38, 4, T), scr(42, 4, T)
        q2, k2z, v2, R2 = scr(46, 4, T), scr(50, 8, T), scr(58, TB, 512), scr(62, 8, T)
        TG, ZT = scr(60, 2, T), scr(62, 2, T)
        UR, UC = scr(30, 4, T + 2), scr(36, 4, T)
        OT, OUT = scr(0, KD, T), scr(8, TB, D)

        par = sb("par", [P, NPAR])
        ident, ones = sb("ident", [P, P]), sb("ones", [P, P])
        identb = sb("identb", [P, P], BF16)
        mask1, mask2 = sb("mask1", [P, 256], BF16), sb("mask2", [P, P], BF16)
        hmask = sb("hmask", [P, C], U32)
        CL, M0, M1, SL, OL, J = (sb(n, [P, P]) for n in ("CL", "M0", "M1", "SL", "OL", "J"))
        UT = sb("UT", [P, P], BF16)
        reset = sb("reset", [P, T], BF16)
        R0, R1, R2a, oR0, oR1 = (sb(n, [P, w]) for n, w in (("R0", TB), ("R1", TB), ("R2a", TB), ("oR0", 8), ("oR1", 8)))
        fetch, fetch2 = sb("fetch", [P, 1]), sb("fetch2", [P, 1])
        acc = sb("acc", [P, W])
        brow = sb("brow", [P, D])
        eps, negb = sb("eps", [P, 1]), sb("negb", [P, 58])
        lb, oml, lbd = (sb(n, [P, 8]) for n in ("lb", "oml", "lbd"))
        cact, mod = sb("cact", [P, 8]), sb("mod", [P, 48])
        am, af = sb("am", [P, 8]), sb("af", [P, 8])
        RM, NM, DS, ES, SU, RD = (sb(n, [P, 2, 8]) for n in ("RM", "NM", "DS", "ES", "SU", "RD"))
        E5 = sb("E5", [P, 4, 4])
        dtH, dtL = sb("dtH", [P, KD, 8], F32R), sb("dtL", [P, KD, 8], F32R)
        DT, DR, DA, DE, ADT = (sb(n, [P, TB, 8]) for n in ("DT", "DR", "DA", "DE", "ADT"))
        nega, Bs = sb("nega", [P, 8]), sb("Bs", [P, 6, 8])
        ext_dram = nc.dram_tensor("ext_dram", (8, 384), F32).ap()

        ps = ctx.enter_context(nc.psum_tensor("ps", [P, 8, 512], F32))
        ss, ss2 = ps[:, 4:6, 0], ps[:, 6:8, 0]
        rb = ps[:, 6, 256:512]
        rb2 = ps[:, 7, 256:512]
        yss, yrb = ps[:, 2:4, 256], ps[:, 3, 256:512]
        adaps = ps[:, 7, 0:4]
        sc45 = ps[:, 4:6, :].rearrange("p b n -> p (b n)")
        pt67 = ps[:, 6:8, :].rearrange("p b n -> p (b n)")

        def pc(name, i=0, n=1):
            return par[:, PAR[name][0] + i:PAR[name][0] + i + n]

        FIRST_USE = ("q0", "ba0", "bh0", "out0", "f0", "down0", "xs", "oo0", "u0", "dd0")
        OPND = {"P1": (p1H, p1L), "PY": (pyH, pyL), "Z": (zH, zL)}

        def operand_ready(name, k):
            if name[:3] == "out":
                return on.merged, 1
            if name[:2] == "ba":
                return on.yT_done, NU1
            if name[:2] == "bh":
                return on.hs_done, k // 4 + 1
            if name[:2] == "oo":
                return (on.snorm_done, 1) if k < 4 else (on.yT_done, 9)
            if name[:4] == "down":
                return on.z_ready, k // 2 + 1
            if name[:2] == "dd":
                return on.z_ready, NF + k // 2 + 1
            return on.u_ready, 8 * ("q0", "f0", "xs", "u0").index(name) + k + 1

        def h_ready(n, k):
            if n == 0:
                return on.x_done, k + 1
            return EV[f"{('out', 'down', 'oo', 'dd')[n - 1]}{k // 4}", k % 4]

        block = ctx.enter_context(nc.Block())

        @block.sync
        def _(sp):
            for b in range(4):
                sp.dma_start(xtok[:, :, b * T:(b + 1) * T],
                             IN["x"][0].rearrange("(j p) n -> p j n", p=P)[:, :, b * T:(b + 1) * T]).then_inc(on.in_x[b], 16)
                if b == 0:
                    sp.dma_start(par[:], IN["params"]).then_inc(on.in_par, 16)
            for i, (kind, q) in enumerate(stream):
                if i >= NRAW:
                    sp.wait_ge(on.w_lo, i - NRAW + 1)
                if kind == "w":
                    name, part = panels[q]
                    g = GROUPS[name]
                    k0, nk = g["parts"][part]
                    off = 0
                    for s, (c0, w) in enumerate(g["seg"]):
                        src = IN[g["w"] if isinstance(g["w"], str) else g["w"][s]][0]
                        src = src.rearrange("(k p) n -> p k n", p=P)[:, k0:k0 + nk, c0:c0 + w]
                        sp.dma_start(raw[:, i % NRAW, 0:nk, off:off + w], src).then_inc(on.raw[i % NRAW], 16)
                        off += w
                else:
                    src = IN["w_ada_2"][0].rearrange("(k p) n -> p k n", p=P)
                    src = src[:, (q % 2) * KP:(q % 2 + 1) * KP, (q // 2) * W:(q // 2 + 1) * W]
                    sp.dma_start(raw[:, i % NRAW, :, :], src).then_inc(on.raw[i % NRAW], 16)
                if i == 2:
                    bi = IN["b_in"]
                    sp.dma_start(brow[:], bi[0:1, 3328:3328 + D].partition_broadcast(P)).then_inc(on.in_brow, 16)
                    sp.dma_start(vrow, bi[0:1, 1152:1152 + P].partition_broadcast(P)).then_inc(on.in_brow, 16)
                    sp.dma_start(dtw, IN["w_in_2"][0].rearrange("(k p) n -> p k n", p=P)[:, :, 1536:1544]).then_inc(on.in_dtw, 16)
                    sp.dma_start(ext[:, P - 1:P - 1 + 257], IN["rel_rev"]).then_inc(on.in_rel, 16)
                if i == 10:
                    sp.wait_ge(on.ext_done, 1)
                    sp.dma_start(ext_dram[:, :], ext).then_inc(on.ext_out, 16)
                if kind == "w" and panels[q] == ("xs", 1):
                    sp.wait_ge(on.ext_out, 16)
                    sp.wait_ge(on.u_ready, 24)
                    sp.dma_start(R2, bass.AP(ext_dram.tensor, 0, [[1, P], [384, 8], [1, T]])).then_inc(on.in_R2, 16)
            for j in range(TB):
                sp.wait_ge(on.out_done, j + 1)
                sp.dma_start(out[0, j * P:(j + 1) * P, :], OUT[:, j, :]).then_inc(on.stored, 16)
            sp.wait_ge(on.stored, 16 * TB)

        @block.gpsimd
        def _(pool):

            steps = [0]

            def step(ins):
                steps[0] += 1
                ins.then_inc(on.pool_step, 1)
                pool.wait_ge(on.pool_step, steps[0])

            def select(t, cond, fill, op=ALU.is_ge):
                base_, mult, stp = cond
                step(pool.affine_select(out=t, in_=t, compare_op=op, fill=fill, base=base_,
                                        pattern=[[stp, t.shape[-1]]], channel_multiplier=mult))

            step(pool.memset(eps[:], EPS))
            step(pool.memset(nega[:], 0.0))
            step(pool.memset(ident[:], 0.0))
            select(ident[:], (0, 1, -1), 1.0, ALU.not_equal)
            step(pool.memset(ones[:], 1.0))
            step(pool.memset(identb[:], 0.0))
            select(identb[:], (0, 1, -1), 1.0, ALU.not_equal)
            step(pool.memset(mask1[:], 0.0))
            select(mask1[:, 0:P], (-1, -1, 1), NEG)
            select(mask1[:, P:2 * P], (0, 1, -1), NEG)
            step(pool.memset(mask2[:], 0.0))
            step(pool.memset(mask2[0:C, C:P], NEG))
            step(pool.memset(reset[:], 1.0))
            step(pool.memset(reset[:, 0:T:C], 0.0))
            step(pool.memset(J[:], 0.0))
            select(J[:], (-(P - 1), 1, 1), 1.0, ALU.not_equal)
            step(pool.memset(UT[:], 1.0))
            select(UT[:], (0, -1, 1), 0.0)
            step(pool.tensor_copy(CL[:], UT[:]))
            step(pool.memset(CL[0:C, C:P], 0.0))
            step(pool.memset(SL[:], 1.0))
            select(SL[:], (-1, 1, -1), 0.0)
            step(pool.memset(OL[:], 0.0))
            step(pool.memset(OL[0:C, :], 1.0))
            step(pool.memset(M0[:], 0.0))
            step(pool.tensor_scalar(M0[:, 0:C], CL[:, 0:C], -1.0, None, ALU.mult))
            step(pool.memset(M1[:], 0.0))
            step(pool.tensor_scalar(M1[:, C:P], CL[:, C:P], -1.0, None, ALU.mult))
            step(pool.tensor_copy(M1[0:C, 0:C], SL[0:C, 0:C]))
            step(pool.tensor_copy(hmask[0:C, :], UT[0:C, 0:C]))
            step(pool.tensor_copy(hmask[C:P, :], UT[C:P, C:P]))
            pool.memset(fetch2[:], 0.0).then_inc(on.consts, 1)

        @block.scalar
        def _(act):

            def split_hi(q):
                i = SIDX["w", q]
                nk = GROUPS[panels[q][0]]["parts"][panels[q][1]][1]
                wd = sum(w for _, w in GROUPS[panels[q][0]]["seg"])
                act.wait_ge(on.raw[i % NRAW], landed[i])
                if q >= NHL:
                    act.wait_ge(*USED[q - NHL])
                nc.scalar.activation(wH[:, q % NHL, 0:nk, 0:wd], raw[:, i % NRAW, 0:nk, 0:wd], ACT.Copy).then_inc(on.w_hi, 1)

            def norm(n):
                nc.scalar.activation(fetch[:], eps[:], ACT.Sqrt).then_inc(on.act_fetch, 1)
                for k in range(KD):
                    act.wait_ge(*h_ready(n, k))
                    nc.scalar.activation(SQ[:, k], hT[:, k], ACT.Square).then_inc(on.sq_done, 1)
                    if n == 2:
                        act.wait_ge(on.hg_done, k + 1)
                        nc.scalar.activation(SQ2[:, k], HG[:, k], ACT.Square).then_inc(on.sq2_done, 1)
                if n == 0:
                    split_hi(0)
                act.wait_ge(on.ss_done, n + 1)
                nc.scalar.activation(R0[:], ss, ACT.Sqrt, scale=1.0 / D, bias=eps[:, 0:1]).then_inc(on.rt_done, 1)
                if n == 2:
                    act.wait_ge(on.ms2_done, 1)
                    nc.scalar.activation(R2a[:], R2a[:], ACT.Sqrt, scale=1.0 / D, bias=eps[:, 0:1]).then_inc(on.rt2_done, 1)
                if n == 4:
                    return
                for k in range(KD):
                    act.wait_ge(on.tmp_done, 8 * n + k + 1)
                    if n < 2:
                        nc.scalar.activation(p1H[:, k], TMP[:, k], ACT.Copy).then_inc(on.uh_done, 1)
                    else:
                        o = (0 if n == 2 else 24) + k
                        nc.scalar.activation(p1H[:, k], TMP[:, k], ACT.Identity,
                                             bias=mod[:, o:o + 1]).then_inc(on.uh_done, 1)
                if n == 0:
                    split_hi(1)

            def evac(name):
                g = name.rstrip("0123456789")
                i = int(name[len(g):] or 0)

                def each(dst, f, **kw):
                    for m, t in enumerate(GROUPS[name]["tiles"]):
                        if GROUPS[name]["evac"][m] == "A":
                            act.wait_ge(on.tile_done, TILE[name, m])
                            bias = {a: b(m) if callable(b) else b for a, b in kw.items()}
                            nc.scalar.activation(dst(m), ps[:, t[1], 0:T], f, **bias).then_inc(on.evac_act, 1)

                if g == "q" and name in ("q0", "q1"):
                    each(lambda m: aQ[:, 4 * i + m], ACT.Identity, bias=lambda m: pc("b_in", 4 * i + m))
                elif name == "kv":
                    each(lambda m: aK, ACT.Identity, bias=lambda m: pc("b_in", 8))
                elif g in ("ga", "gb"):
                    b0, G = (42, GA) if g == "ga" else (50, GB)
                    each(lambda m: G[:, 4 * i + m], ACT.Sigmoid, bias=lambda m: pc("b_in", b0 + 4 * i + m))
                elif g == "hq":
                    act.wait_ge(on.ext_out, 16)
                    if i:
                        act.wait_ge(on.o_psum, 2 * i)
                        act.wait_ge(on.hfin, i)
                    for m in range(4):
                        act.wait_ge(on.tile_done, TILE[name, m])
                        nc.scalar.activation(T1[:, m], ps[:, m, 0:T], ACT.Sigmoid,
                                             bias=pc("b_in", 10 + 4 * i + m)).then_inc(on.sig_part, 1)
                        nc.scalar.activation(hQ[:, m], ps[:, m, 0:T], ACT.Identity,
                                             bias=pc("b_in", 10 + 4 * i + m)).then_inc(on.evac_act, 1)
                elif g == "hf":
                    act.wait_ge(on.hq_done, i + 1)
                    for m in range(4):
                        act.wait_ge(on.tile_done, TILE[name, m])
                        nc.scalar.activation(T1[:, m], ps[:, m, 0:T], ACT.Sigmoid,
                                             bias=pc("b_in", 18 + 4 * i + m)).then_inc(on.sig_part, 1)
                        nc.scalar.activation(T2[:, m], ps[:, m, 0:T], ACT.Sigmoid, scale=-1.0,
                                             bias=negb[:, 18 + 4 * i + m:19 + 4 * i + m]).then_inc(on.evac_act, 1)
                    act.wait_ge(on.evac_act, EV[name, 3][1])
                    act.wait_ge(on.lb_sig, 2)
                    for h in range(4):
                        nc.scalar.activation(hB[:, h], T1[:, h], ACT.Ln, scale=oml[:, 4 * i + h:4 * i + h + 1],
                                             bias=lb[:, 4 * i + h:4 * i + h + 1]).then_inc(on.hf_log, 1)
                elif g == "hg":
                    if i:
                        act.wait_ge(on.hfin, i)
                    each(lambda m: hG[:, m], ACT.Sigmoid, bias=lambda m: pc("b_in", 34 + 4 * i + m))
                elif g == "f":
                    each(lambda m: TG[:, m], ACT.Silu)
                    act.wait_ge(on.evac_dve, EV[name, 3][1])
                    nc.scalar.activation(zH[:, 2 * i:2 * i + 2], ZT, ACT.Copy).then_inc(on.zh_done, 1)
                elif g in ("xs", "bc"):
                    if g == "bc":
                        act.wait_ge(on.conv_done, 12)
                    act.wait_ge(on.xr_zero, 1)
                    each(lambda m: XR[:, m, 3:T + 3], ACT.Copy)
                    act.wait_ge(on.evac_act, EV[name, 3][1])
                    s = int(g == "bc")
                    for m in range(4):
                        nc.scalar.activation(XC[:, 4 * s + m], XR[:, m, 0:T], ACT.Identity, scale=pc("conv_w", 4 * s + m), bias=pc("conv_b", 4 * s + m)).then_inc(on.conv0, 1)
                    act.wait_ge(on.conv_done, 12 * s + 12)
                    nc.scalar.activation(XC[:, 4 * s:4 * s + 4], XC[:, 4 * s:4 * s + 4], ACT.Silu).then_inc(on.xc_done, 1)
                elif name == "q2":
                    each(lambda m: q2[:, m], ACT.Copy, scale=0.125)
                elif name == "k2":
                    act.wait_ge(on.kz_zero, 1)
                    for m in range(4):
                        act.wait_ge(on.tile_done, TILE[name, m])
                        nc.scalar.activation(k2z[0:C, 2 * m], ps[0:C, m, 0:T], ACT.Copy).then_inc(on.k2_half, 1)
                        nc.scalar.activation(k2z[C:P, 2 * m + 1], ps[C:P, m, 0:T], ACT.Copy).then_inc(on.evac_act, 1)
                elif name == "z":
                    each(lambda m: sZ[:, m], ACT.Silu)
                elif g == "u":
                    act.wait_ge(on.ur_zero, 1)
                    if i:
                        act.wait_ge(on.uconv_done, 8 * i)
                    each(lambda m: UR[:, m, 2:T + 2], ACT.Copy)
                    act.wait_ge(on.evac_act, EV[name, 3][1])
                    for m in range(4):
                        wi = 2 * i + m % 2 + (KF if m > 1 else 0)
                        nc.scalar.activation(UC[:, m], UR[:, m, 0:T], ACT.Identity, scale=pc("ffn_conv_w", wi)).then_inc(on.uconv0, 1)
                    act.wait_ge(on.uconv_done, 8 * i + 8)
                    nc.scalar.activation(UC[:, 0:2], UC[:, 0:2], ACT.Silu).then_inc(on.u_silu, 1)
                    act.wait_ge(on.zt_done, i + 1)
                    nc.scalar.activation(zH[:, 2 * i:2 * i + 2], ZT, ACT.Copy).then_inc(on.zh_done, 1)

            act.wait_ge(on.in_par, 16)
            act.wait_ge(on.pool_step, 2)
            act.wait_ge(on.lb_diff, 1)
            nc.scalar.activation(oml[:], lbd[:], ACT.Sigmoid, scale=-1.0).then_inc(on.lb_sig, 1)
            nc.scalar.activation(lb[:], lbd[:], ACT.Sigmoid).then_inc(on.lb_sig, 1)
            nc.scalar.activation(cact[:], pc("c", 0, 8), ACT.Silu).then_inc(on.c_silu, 1)
            nc.scalar.activation(nega[:], pc("a_log", 0, 8), ACT.Exp).then_inc(on.a_exp, 1)
            for e in TL:
                k = e[0]
                if k == "panel":
                    q = PIDX[e[1:]] + AHEAD
                    if q < len(panels):
                        split_hi(q)
                elif k == "norm":
                    norm(e[1])
                elif k == "evac":
                    evac(e[1])
                elif k == "setup":
                    act.wait_ge(on.in_dtw, 16)
                    nc.scalar.activation(dtH[:], dtw, ACT.Copy).then_inc(on.dtw_hi, 1)
                elif k == "scores":
                    u = e[1]
                    kind, n, h0, nh, nk = UNITS[u]
                    act.wait_ge(on.negmax, u + 1)
                    act.wait_ge(on.scores_done, u + 1)
                    if u:
                        act.wait_ge(on.pt_psum, u)
                        act.wait_ge(on.pv_done, u - 1)
                    scale = 0.125 if kind == 1 else 1.0
                    for h in range(nh):
                        nc.scalar.activation(PR[:, h * nk:(h + 1) * nk, :], sc45[:, h * nk * P:(h + 1) * nk * P].rearrange("p (a b) -> p a b", b=P), ACT.Exp, scale=scale, bias=NM[:, u % 2, h:h + 1], accum_out=SU[:, u % 2, h:h + 1]).then_inc(on.probs if h == nh - 1 else on.probs_part, 1)
                    if kind == 1:
                        act.wait_ge(on.dsink, u + 1)
                        nc.scalar.activation(ES[:, u % 2, 0:nh], DS[:, u % 2, 0:nh], ACT.Exp).then_inc(on.esink, 1)
                elif k == "pt":
                    u = e[1]
                    act.wait_ge(on.pt_psum, u + 1)
                    if u:
                        act.wait_ge(on.pv_psum, u)
                    nc.scalar.activation(PT[:, 0:4], pt67[:, 0:512].rearrange("p (a b) -> p a b", b=P), ACT.Copy).then_inc(on.pt_part, 1)
                    nc.scalar.activation(PT[:, 4:8], pt67[:, 512:1024].rearrange("p (a b) -> p a b", b=P), ACT.Copy).then_inc(on.pt_done, 1)
                elif k == "yT":
                    u = e[1]
                    kind, n, h0, nh, nk = UNITS[u]
                    b0, nb = h0 // 2 + (4 if kind == 2 else 0), nh // 2
                    act.wait_ge(on.yT_psum, u + 1)
                    nc.scalar.activation(pyH[:, b0:b0 + nb, n * P:(n + 1) * P], ps[:, 4, 0:nb * P].rearrange("p (a b) -> p a b", b=P), ACT.Copy).then_inc(on.yTh, 1)
                elif k == "hprep":
                    s = e[1]
                    if e[2] == 0:
                        act.wait_ge(on.hdm, s + 1)
                        nc.scalar.activation(T2, T1, ACT.Exp).then_inc(on.hE1, 1)
                    elif e[2] == 1:
                        act.wait_ge(on.hE1, s + 1)
                        nc.scalar.activation(T1, T1, ACT.Exp, scale=-1.0).then_inc(on.hE2, 1)
                    elif e[2] == 2:
                        act.wait_ge(on.hQp, s + 1)
                        nc.scalar.activation(T2, hB, ACT.Exp).then_inc(on.hE3, 1)
                        nc.scalar.activation(E5[:], hB[:, :, C - 1:T:C], ACT.Exp).then_inc(on.hE5, 1)
                    else:
                        act.wait_ge(on.hdl, s + 1)
                        nc.scalar.activation(T1, T1, ACT.Exp).then_inc(on.hE4, 1)
                elif k == "hA":
                    s = e[1]
                    act.wait_ge(on.hkt_psum, s + 1)
                    for j in range(TB):
                        nc.scalar.activation(hKT[:, j], ps[:, 5 + j, :], ACT.Copy).then_inc(on.hkt, 1)
                elif k == "hC":
                    s = e[1]
                    for j in range(TB):
                        act.wait_ge(on.o_psum, 2 * s + j + 1)
                        v = ps[:, 4 + 3 * j, :].rearrange("p (h n) -> p h n", h=4)
                        nc.scalar.activation(T1[:, :, j * P:(j + 1) * P], v, ACT.Copy).then_inc(on.o_copy, 1)
                        nc.scalar.activation(T2[:, :, j * P:(j + 1) * P], v, ACT.Square).then_inc(on.o_sq, 1)
                elif k == "hD":
                    s = e[1]
                    act.wait_ge(on.oss_psum, s + 1)
                    nc.scalar.activation(oR0[:], ps[:, 5, 0:8], ACT.Sqrt, scale=1.0 / P,
                                         bias=eps[:, 0:1]).then_inc(on.o_rt, 1)
                elif k == "hsplit":
                    s = e[1]
                    act.wait_ge(on.hfin, s + 1)
                    act.wait_ge(*USED[PIDX["ba1", 1]])
                    nc.scalar.activation(pyH[:, 4 * s:4 * s + 4], YF0 if s == 0 else T1, ACT.Copy).then_inc(on.hsh, 1)
                elif k == "merge":
                    act.wait_ge(on.mixed, 8)
                    nc.scalar.activation(p1H[:], GA, ACT.Copy).then_inc(on.mh, 1)
                elif k == "dt":
                    act.wait_ge(on.dt_abs, 1)
                    nc.scalar.activation(DE[:], DA[:], ACT.Exp).then_inc(on.dt_e, 1)
                    act.wait_ge(on.dt_e, 1)
                    nc.scalar.activation(DE[:], DE[:], ACT.Ln, bias=1.0).then_inc(on.dt_ln, 1)
                elif k == "sA":
                    act.wait_ge(on.seg, e[1] + 1)
                    nc.scalar.activation(SG, SG, ACT.Exp).then_inc(on.seg_exp, 1)
                elif k == "snorm":
                    act.wait_ge(on.yz, 1)
                    nc.scalar.activation(sT, sY, ACT.Square).then_inc(on.ysq, 1)
                    act.wait_ge(on.yss, 1)
                    nc.scalar.activation(R0[:], yss, ACT.Sqrt, scale=1.0 / 512, bias=eps[:, 0:1]).then_inc(on.yrt, 1)
                    act.wait_ge(on.ytmp, 1)
                    nc.scalar.activation(pyH[:, 0:4], sY, ACT.Copy).then_inc(on.snh, 1)
                elif k == "store":
                    for j in range(TB):
                        for b in range(2):
                            act.wait_ge(on.ot_psum, 2 * j + b + 1)
                            nc.scalar.activation(OUT[:, j, b * 512:(b + 1) * 512], ps[:, 4 + 2 * j + b, :], ACT.Copy).then_inc(on.out_done if b else on.out_part, 1)

        @block.vector
        def _(dve):
            v = nc.vector

            steps = [0]

            def step(ins):
                steps[0] += 1
                ins.then_inc(on.dve_step, 1)
                dve.wait_ge(on.dve_step, steps[0])

            def tt(o, a, b, op):
                return v.tensor_tensor(o, a, b, op)

            def stt(o, a, s, b, op0, op1):
                return v.scalar_tensor_tensor(out=o, in0=a, scalar=s, in1=b, op0=op0, op1=op1)

            def split_lo(q):
                i = SIDX["w", q]
                nk = GROUPS[panels[q][0]]["parts"][panels[q][1]][1]
                wd = sum(w for _, w in GROUPS[panels[q][0]]["seg"])
                dve.wait_ge(on.w_hi, q + 1)
                tt(wL[:, q % NHL, 0:nk, 0:wd], raw[:, i % NRAW, 0:nk, 0:wd],
                       wH[:, q % NHL, 0:nk, 0:wd].bitcast(F32), ALU.subtract).then_inc(on.w_lo, 1)

            def norm(n):
                if n == 2:
                    for k in range(KD):
                        dve.wait_ge(*h_ready(n, k))
                        v.tensor_scalar(HG[:, k], hT[:, k], pc("norm_final_g", k), None, ALU.mult).then_inc(on.hg_done, 1)
                if n == 0:
                    split_lo(0)
                dve.wait_ge(on.rt_done, n + 1)
                v.reciprocal(R1[:], R0[:]).then_inc(on.rd_done, 1)
                src, gain = hT, {0: lambda k: pc("norm_mix_g", k), 1: lambda k: pc("norm_ffn_g", k),
                                 3: lambda k: af[:, k:k + 1], 4: lambda k: pc("final_norm_w", k)}.get(n)
                if n == 2:
                    dve.wait_ge(on.rd_done, n + 1)
                    step(tt(R2a[:], R1[:], R1[:], ALU.mult))
                    tt(R2a[:], ss2, R2a[:], ALU.mult).then_inc(on.ms2_done, 1)
                    dve.wait_ge(on.rt2_done, 1)
                    step(v.reciprocal(R2a[:], R2a[:]))
                    tt(R2a[:], R2a[:], R1[:], ALU.mult).then_inc(on.rd2_done, 1)
                    src, gain = HG, lambda k: am[:, k:k + 1]
                dve.wait_ge(on.bcast, n + 1)
                if n == 4:
                    for k in range(KD):
                        stt(OT[:, k], hT[:, k], gain(k), rb, ALU.mult, ALU.mult).then_inc(on.ot_done, 1)
                    return

                def low(k):
                    dve.wait_ge(on.uh_done, 8 * n + k + 1)
                    if n < 2:
                        tt(p1L[:, k], TMP[:, k], p1H[:, k].bitcast(F32), ALU.subtract).then_inc(on.u_ready, 1)
                    else:
                        o = (0 if n == 2 else 24) + k
                        stt(p1L[:, k], TMP[:, k], mod[:, o:o + 1], p1H[:, k].bitcast(F32), ALU.add,
                            ALU.subtract).then_inc(on.u_ready, 1)
                for k in range(KD):
                    stt(TMP[:, k], src[:, k], gain(k), rb, ALU.mult, ALU.mult).then_inc(on.tmp_done, 1)
                    if k >= 2:
                        low(k - 2)
                low(KD - 2)
                low(KD - 1)
                if n == 0:
                    split_lo(1)
                if n == 2:
                    for k in range(KD):
                        tt(hT[:, k], HG[:, k], rb2, ALU.mult).then_inc(on.h_final, 1)

            def evac(name):
                g = name.rstrip("0123456789")
                i = int(name[len(g):] or 0)
                if name in ("q0", "q1", "q2"):
                    return
                if name == "kv":
                    dve.wait_ge(on.evac_act, EV[name, 0][1])
                    for gr in range(2):
                        for b in range(2):
                            v.tensor_copy(aKZ[C * b:C * b + C, 2 * gr + b], aK[C * gr:C * gr + C]).then_inc(on.kz, 1)
                            dve.wait_ge(on.kz, 2 * gr + b + 1)
                    dve.wait_ge(on.in_brow, 32)
                    for j in range(TB):
                        dve.wait_ge(on.tile_done, TILE[name, 1 + j])
                        tt(aV[:, j], ps[:, 2 + j, 0:P], vrow, ALU.add).then_inc(on.evac_dve, 1)
                elif g == "hq":
                    dve.wait_ge(on.evac_act, EV[name, 3][1])
                    tt(hQ, hQ, T1, ALU.mult).then_inc(on.hq_done, 1)
                elif g == "hf":
                    dve.wait_ge(on.lb_sig, 2)
                    for h in range(4):
                        dve.wait_ge(on.evac_act, EV[name, h][1])
                        v.tensor_scalar(hK[:, h], T2[:, h], oml[:, 4 * i + h:4 * i + h + 1], None,
                                        ALU.mult).then_inc(on.hk_done, 1)
                    for h in range(4):
                        dve.wait_ge(on.hf_log, 4 * i + h + 1)
                        v.tensor_tensor_scan(hB[:, h], reset[:], hB[:, h], 0.0, ALU.mult, ALU.add).then_inc(on.hb_done, 1)
                elif g == "hi":
                    if i:
                        dve.wait_ge(on.o_psum, 2 * i)
                    for j in range(TB):
                        dve.wait_ge(on.tile_done, TILE[name, j])
                        tt(hV[:, j], ps[:, 2 + j, :], brow[:, i * W:(i + 1) * W], ALU.add).then_inc(on.evac_dve, 1)
                elif g == "ba":
                    for m in range(4):
                        dve.wait_ge(on.tile_done, TILE[name, m])
                        tt(GA[:, 4 * i + m], ps[:, m, 0:T], GA[:, 4 * i + m], ALU.mult).then_inc(on.evac_dve, 1)
                elif g == "bh":
                    for m in range(4):
                        dve.wait_ge(on.tile_done, TILE[name, m])
                        tt(GB[:, 4 * i + m], ps[:, m, 0:T], GB[:, 4 * i + m], ALU.mult).then_inc(on.evac_dve, 1)
                        dve.wait_ge(on.evac_dve, EV[name, m][1])
                        tt(GA[:, 4 * i + m], GB[:, 4 * i + m], GA[:, 4 * i + m], ALU.add).then_inc(on.mixed, 1)
                elif g in ("out", "down"):
                    for m in range(4):
                        dve.wait_ge(on.tile_done, TILE[name, m])
                        tt(hT[:, 4 * i + m], ps[:, m, 0:T], hT[:, 4 * i + m], ALU.add).then_inc(on.evac_dve, 1)
                elif g in ("oo", "dd"):
                    for m in range(4):
                        o = (16 if g == "oo" else 40) + 4 * i + m
                        dve.wait_ge(on.tile_done, TILE[name, m])
                        stt(hT[:, 4 * i + m], ps[:, m, 0:T], mod[:, o:o + 1], hT[:, 4 * i + m], ALU.mult, ALU.add).then_inc(on.evac_dve, 1)
                elif g == "f":
                    dve.wait_ge(on.z_ready, i)
                    for m in range(2):
                        dve.wait_ge(on.tile_done, TILE[name, 2 + m])
                        dve.wait_ge(on.evac_act, EV[name, m][1])
                        tt(ZT[:, m], ps[:, 2 + m, 0:T], TG[:, m], ALU.mult).then_inc(on.evac_dve, 1)
                    dve.wait_ge(on.zh_done, i + 1)
                    tt(zL[:, 2 * i:2 * i + 2], ZT, zH[:, 2 * i:2 * i + 2].bitcast(F32), ALU.subtract).then_inc(on.z_ready, 1)
                elif g in ("xs", "bc"):
                    s = int(g == "bc")
                    for tap in range(1, 4):
                        for m in range(4):
                            dve.wait_ge(on.conv0, 4 * s + m + 1)
                            dve.wait_ge(on.conv_done, 12 * s + max(4 * (tap - 2) + m + 1, 0))
                            stt(XC[:, 4 * s + m], XR[:, m, tap:tap + T], pc("conv_w", 8 * tap + 4 * s + m),
                                XC[:, 4 * s + m], ALU.mult, ALU.add).then_inc(on.conv_done, 1)
                elif name == "v2":
                    for j in range(TB):
                        dve.wait_ge(on.tile_done, TILE[name, j])
                        v.tensor_copy(v2[:, j], ps[:, 2 + j, :]).then_inc(on.evac_dve, 1)
                elif g == "u":
                    for tap in range(1, 3):
                        for m in range(4):
                            wi = KF * 2 * tap + 2 * i + m % 2 + (KF if m > 1 else 0)
                            dve.wait_ge(on.uconv0, 4 * i + m + 1)
                            if tap == 2:
                                dve.wait_ge(on.uconv_done, 8 * i + m + 1)
                            stt(UC[:, m], UR[:, m, tap:tap + T], pc("ffn_conv_w", wi), UC[:, m], ALU.mult,
                                ALU.add).then_inc(on.uconv_done, 1)
                    dve.wait_ge(on.uconv_done, 8 * i + 8)
                    dve.wait_ge(on.u_silu, i + 1)
                    dve.wait_ge(on.z_ready, NF + i)
                    tt(ZT, UC[:, 0:2], UC[:, 2:4], ALU.mult).then_inc(on.zt_done, 1)
                    dve.wait_ge(on.zt_done, i + 1)
                    dve.wait_ge(on.zh_done, NF + i + 1)
                    tt(zL[:, 2 * i:2 * i + 2], ZT, zH[:, 2 * i:2 * i + 2].bitcast(F32), ALU.subtract).then_inc(on.z_ready, 1)

            dve.wait_ge(on.in_par, 16)
            tt(lbd[:], pc("lb0", 0, 8), pc("lb1", 0, 8), ALU.subtract).then_inc(on.lb_diff, 1)
            dve.wait_ge(on.a_exp, 1)
            step(v.tensor_scalar(nega[:], nega[:], -1.0, None, ALU.mult))
            v.tensor_scalar(negb[:], pc("b_in", 0, 58), -1.0, None, ALU.mult).then_inc(on.negb, 1)
            dve.wait_ge(on.negb, 1)
            for e in TL:
                k = e[0]
                if k == "load_x":
                    for b in range(4):
                        dve.wait_ge(on.x_psum, b + 1)
                        for kk in range(2):
                            v.tensor_copy(hT[:, 2 * b + kk], ps[:, 4 + b, kk * T:(kk + 1) * T]).then_inc(on.x_done, 1)
                elif k == "panel":
                    q = PIDX[e[1:]] + AHEAD
                    if q < len(panels):
                        split_lo(q)
                elif k == "norm":
                    norm(e[1])
                elif k == "evac":
                    evac(e[1])
                elif k == "setup":
                    step(v.memset(aKZ, 0.0))
                    dve.wait_ge(on.in_rel, 16)
                    step(v.memset(ext[:, 0:P - 1], 0.0))
                    v.tensor_scalar(ext[:, 0:P - 1], ext[:, 0:P - 1], ext[:, P - 1:P], None, ALU.add).then_inc(on.ext_done, 1)
                    dve.wait_ge(on.dtw_hi, 1)
                    tt(dtL[:], dtw, dtH[:].bitcast(F32), ALU.subtract).then_inc(on.dtw_lo, 1)
                elif k == "ada":
                    q = e[1]
                    i = SIDX["ada", q]
                    dve.wait_ge(on.raw[i % NRAW], landed[i])
                    if q % 2 == 0 and q:
                        dve.wait_ge(on.ada_psum, q // 2)
                    if q == 0:
                        dve.wait_ge(on.c_silu, 1)
                    for kk in range(KP):
                        c = cact[:, (q % 2) * KP + kk:(q % 2) * KP + kk + 1]
                        if kk == 0 and q % 2 == 0:
                            ins = v.tensor_scalar(acc[:], raw[:, i % NRAW, kk], c, None, ALU.mult)
                        else:
                            ins = stt(acc[:], raw[:, i % NRAW, kk], c, acc[:], ALU.mult, ALU.add)
                        if kk < KP - 1:
                            step(ins)
                    ins.then_inc(on.w_lo, 1)
                    dve.wait_ge(on.w_lo, i + 1)
                elif k == "ada_sum":
                    q = e[1]
                    dve.wait_ge(on.ada_psum, q + 1)
                    tt(mod[:, 4 * q:4 * q + 4], adaps, pc("b_ada", 4 * q, 4), ALU.add).then_inc(on.ada_done, 1)
                elif k == "mod":
                    dve.wait_ge(on.ada_done, 12)
                    step(stt(am[:], mod[:, 8:16], 1.0, pc("norm_mix_w_2", 0, 8), ALU.add, ALU.mult))
                    step(stt(af[:], mod[:, 32:40], 1.0, pc("norm_ffn_w_2", 0, 8), ALU.add, ALU.mult))
                elif k == "scores":
                    u = e[1]
                    kind, n, h0, nh, nk = UNITS[u]
                    pu = u % 2
                    dve.wait_ge(on.scores_done, u + 1)
                    if u > 1:
                        dve.wait_ge(on.probs, u - 1)
                    step(v.reduce_max(RM[:, pu, 0:nh], sc45[:, 0:nh * nk * P].rearrange("p (h k) -> p h k", h=nh), AX_X))
                    if kind == 1:
                        step(stt(RM[:, pu, 0:nh], RM[:, pu, 0:nh], 0.125, pc("sinks", h0, nh), ALU.mult, ALU.max))
                    v.tensor_scalar(NM[:, pu, 0:nh], RM[:, pu, 0:nh], -1.0, None, ALU.mult).then_inc(on.negmax, 1)
                    dve.wait_ge(on.negmax, u + 1)
                    if kind == 1:
                        tt(DS[:, pu, 0:nh], NM[:, pu, 0:nh], pc("sinks", h0, nh), ALU.add).then_inc(on.dsink, 1)
                        dve.wait_ge(on.dsink, u + 1)
                    dve.wait_ge(on.probs, u + 1)
                    if kind == 1:
                        dve.wait_ge(on.esink, u + 1)
                        step(tt(SU[:, pu, 0:nh], SU[:, pu, 0:nh], ES[:, pu, 0:nh], ALU.add))
                    step(v.reciprocal(RD[:, pu, 0:nh], SU[:, pu, 0:nh]))
                elif k == "pv":
                    u = e[1]
                    kind, n, h0, nh, nk = UNITS[u]
                    dve.wait_ge(on.pv_psum, u + 1)
                    if u:
                        dve.wait_ge(on.yT_psum, u)
                    tt(YT[:, 0:nh * DH].rearrange("p (h d) -> p h d", h=nh),
                           ps[:, 6, 0:nh * DH].rearrange("p (h d) -> p h d", h=nh),
                           RD[:, u % 2, 0:nh].unsqueeze(2).broadcast_to([P, nh, DH]), ALU.mult).then_inc(on.pv_done, 1)
                elif k == "yT":
                    u = e[1]
                    kind, n, h0, nh, nk = UNITS[u]
                    b0, nb = h0 // 2 + (4 if kind == 2 else 0), nh // 2
                    dve.wait_ge(on.yTh, u + 1)
                    tt(pyL[:, b0:b0 + nb, n * P:(n + 1) * P],
                           ps[:, 4, 0:nb * P].rearrange("p (a b) -> p a b", b=P),
                           pyH[:, b0:b0 + nb, n * P:(n + 1) * P].bitcast(F32), ALU.subtract).then_inc(on.yT_done, 1)
                elif k == "hprep":
                    s = e[1]
                    bc = hB.rearrange("p h n -> p (h n)").rearrange("p (c n) -> p c n", n=C)
                    f = lambda t: t.rearrange("p h n -> p (h n)").rearrange("p (c n) -> p c n", n=C)
                    if e[2] == 0:
                        dve.wait_ge(on.hb_done, 4 * s + 4)
                        dve.wait_ge(on.hk_done, 4 * s + 4)
                        tt(f(T1), bc, bc[:, :, C // 2 - 1:C // 2].broadcast_to([P, 16, C]), ALU.subtract).then_inc(on.hdm, 1)
                    elif e[2] == 1:
                        if s == 0:
                            dve.wait_ge(on.scores_done, NU1)
                        dve.wait_ge(on.hE1, s + 1)
                        tt(hQp, hQ, T2, ALU.mult).then_inc(on.hQp, 1)
                        dve.wait_ge(on.hE2, s + 1)
                        tt(hKp, hK, T1, ALU.mult).then_inc(on.hKp, 1)
                    elif e[2] == 2:
                        dve.wait_ge(on.hKp, s + 1)
                        tt(f(T1), bc[:, :, C - 1:C].broadcast_to([P, 16, C]), bc, ALU.subtract).then_inc(on.hdl, 1)
                        dve.wait_ge(on.hE3, s + 1)
                        dve.wait_ge(on.hQp, s + 1)
                        tt(hQ, hQ, T2, ALU.mult).then_inc(on.hQq, 1)
                    else:
                        dve.wait_ge(on.hE4, s + 1)
                        tt(hK, hK, T1, ALU.mult).then_inc(on.hKk, 1)
                elif k == "hA":
                    s = e[1]
                    if s == 0:
                        dve.wait_ge(on.kz, 4)
                    step(v.memset(hAT, 0.0))
                    dve.wait_ge(on.hat_psum, s + 1)
                    for c in range(2):
                        r = slice(C * c, C * c + C)
                        v.copy_predicated(hAT[r, :, r], hmask[r, :].unsqueeze(1).broadcast_to([C, 8, C]),
                                              ps[r, 4, :].rearrange("p (a b) -> p a b", b=C)).then_inc(on.hat, 1)
                elif k == "hB":
                    s = e[1]
                    bank = (7, 5, 6)
                    dve.wait_ge(on.hE5, s + 1)
                    dve.wait_ge(on.hkv_psum, 3 * s + 1)
                    v.tensor_copy(hS[:, 0], ps[:, 7, :]).then_inc(on.hS, 1)
                    dve.wait_ge(on.hS, 9 * s + 1)
                    for c in (1, 2):
                        dve.wait_ge(on.hkv_psum, 3 * s + c + 1)
                        for h in range(4):
                            cs = slice(h * P, h * P + P)
                            ins = stt(hS[:, c, cs], hS[:, c - 1, cs], E5[:, h, c:c + 1], ps[:, bank[c], cs], ALU.mult,
                                      ALU.add)
                            ins.then_inc(on.hS, 1)
                        dve.wait_ge(on.hS, 9 * s + 4 * c + 1)
                elif k == "hD":
                    s = e[1]
                    dve.wait_ge(on.o_rt, s + 1)
                    v.reciprocal(oR1[:], oR0[:]).then_inc(on.o_rd, 1)
                    dve.wait_ge(on.o_bcast, s + 1)
                    step(tt(T1.rearrange("p h n -> p (h n)").rearrange("p (b n) -> p b n", b=2),
                            T1.rearrange("p h n -> p (h n)").rearrange("p (b n) -> p b n", b=2), ps[:, 5:7, :], ALU.mult))
                    for h in range(4):
                        ins = stt((YF0 if s == 0 else T1)[:, h], T1[:, h], pc("hgrn_norm_g", 4 * s + h), hG[:, h],
                                  ALU.mult, ALU.mult)
                        if h < 3:
                            step(ins)
                    ins.then_inc(on.hfin, 1)
                    dve.wait_ge(on.hfin, s + 1)
                elif k == "hsplit":
                    s = e[1]
                    dve.wait_ge(on.hsh, s + 1)
                    tt(pyL[:, 4 * s:4 * s + 4], YF0 if s == 0 else T1, pyH[:, 4 * s:4 * s + 4].bitcast(F32),
                           ALU.subtract).then_inc(on.hs_done, 1)
                elif k == "merge":
                    dve.wait_ge(on.mh, 1)
                    tt(p1L[:], GA, p1H[:].bitcast(F32), ALU.subtract).then_inc(on.merged, 1)
                elif k == "dt":
                    dve.wait_ge(on.dt_psum, 1)
                    f = lambda n: pc(n, 0, 8).unsqueeze(1).broadcast_to([P, TB, 8])
                    step(tt(DT[:], ps[:, 7, 0:16].rearrange("p (j h) -> p j h", j=TB), f("dt_bias"), ALU.add))
                    step(v.tensor_scalar(DR[:], DT[:], -1.0, None, ALU.mult))
                    tt(DA[:], DT[:], DR[:], ALU.min).then_inc(on.dt_abs, 1)
                    dve.wait_ge(on.dt_abs, 1)
                    step(v.tensor_scalar(DR[:], DT[:], 0.0, None, ALU.max))
                    dve.wait_ge(on.dt_ln, 1)
                    step(tt(DT[:], DR[:], DE[:], ALU.add))
                    tt(ADT[:], DT[:], nega[:].unsqueeze(1).broadcast_to([P, TB, 8]), ALU.mult).then_inc(on.adt, 1)
                    dve.wait_ge(on.adt, 1)
                    v.memset(k2z, 0.0).then_inc(on.kz_zero, 1)
                    dve.wait_ge(on.kz_zero, 1)
                elif k == "xdt":
                    for j in range(TB):
                        dve.wait_ge(on.xd_psum, j + 1)
                        tt(XD[:, j].rearrange("p (h d) -> p h d", h=8),
                               ps[:, 6 + j, :].rearrange("p (h d) -> p h d", h=8),
                               DT[:, j].unsqueeze(2).broadcast_to([P, 8, DH]), ALU.mult).then_inc(on.xd, 1)
                elif k == "sA":
                    g = e[1]
                    if g == 0:
                        dve.wait_ge(on.bm_psum, 1)
                        step(v.tensor_copy(Bs[:], ps[:, 7, 64:112].rearrange("p (a b) -> p a b", b=8)))
                    dve.wait_ge(on.abc_psum, g + 1)
                    if g:
                        dve.wait_ge(on.sy_psum, g)
                    for x in range(6):
                        c = x if x < 4 else x - 2
                        step(tt(SG[:, :, x * C:(x + 1) * C],
                                sc45.rearrange("p (h n) -> p h n", h=4)[:, :, c * C:(c + 1) * C],
                                Bs[:, x, 4 * g:4 * g + 4].unsqueeze(2).broadcast_to([P, 4, C]), ALU.add))
                    v.tensor_scalar(SG, SG, 0.0, None, ALU.min).then_inc(on.seg, 1)
                    dve.wait_ge(on.seg, g + 1)
                    dve.wait_ge(on.cb_psum, g + 1)
                    step(tt(CB[:, 0:P], ps[:, 6, 0:P], UT[:], ALU.mult))
                    step(v.tensor_copy(CB[:, P:T], ps[:, 6, P:T]))
                    tt(CB[:, T:T + P], ps[:, 6, T:T + P], UT[:], ALU.mult).then_inc(on.cb, 1)
                    dve.wait_ge(on.cb, g + 1)
                    dve.wait_ge(on.seg_exp, g + 1)
                    tt(SG, SG, CB.unsqueeze(1).broadcast_to([P, 4, 384]), ALU.mult).then_inc(on.g_done, 1)
                    dve.wait_ge(on.g_done, g + 1)
                elif k == "sY":
                    g = e[1]
                    dve.wait_ge(on.sy_psum, g + 1)
                    for t in range(2):
                        stt(sY[:, 2 * g + t], XC[:, 2 * g + t], pc("d_skip", 2 * g + t),
                                 ps[:, 7, t * T:(t + 1) * T], ALU.mult, ALU.add).then_inc(on.sy, 1)
                        dve.wait_ge(on.sy, 2 * g + t + 1)
                elif k == "snorm":
                    tt(sY, sY, sZ, ALU.mult).then_inc(on.yz, 1)
                    dve.wait_ge(on.yz, 1)
                    dve.wait_ge(on.yrt, 1)
                    v.reciprocal(R1[:], R0[:]).then_inc(on.yrd, 1)
                    dve.wait_ge(on.ybcast, 1)
                    for t in range(4):
                        ins = stt(sY[:, t], sY[:, t], pc("ssd_norm_w", t), yrb, ALU.mult, ALU.mult)
                        if t < 3:
                            step(ins)
                    ins.then_inc(on.ytmp, 1)
                    dve.wait_ge(on.ytmp, 1)
                    dve.wait_ge(on.snh, 1)
                    tt(pyL[:, 0:4], sY, pyH[:, 0:4].bitcast(F32), ALU.subtract).then_inc(on.snorm_done, 1)
                if k == "norm" and e[1] == 2:
                    v.memset(XR[:, :, 0:3], 0.0).then_inc(on.xr_zero, 1)
                if k == "norm" and e[1] == 3:
                    v.memset(UR[:, :, 0:2], 0.0).then_inc(on.ur_zero, 1)

        @block.tensor
        def _(pe):
            mm = nc.tensor.matmul

            def tr(o, i):
                return nc.tensor.transpose(o, i, ident[:])

            def spread(o, column):
                return mm(o, column.broadcast_to([P, P]), ident[:], start=True, stop=True)

            latest, ada_sums = [None], [0]

            def banks_read():
                if latest[0]:
                    n = len(GROUPS[latest[0]]["tiles"])
                    pe.wait_ge(*EV[latest[0], n - 2])
                    pe.wait_ge(*EV[latest[0], n - 1])

            def panel(name, part):
                q = PIDX[name, part]
                g = GROUPS[name]
                k0, nk = g["parts"][part]
                aH, aL = OPND[g["act"]]
                slot = q % NHL
                final = part == len(g["parts"]) - 1
                pe.wait_ge(on.w_lo, SIDX["w", q] + 1)
                if part == 0:
                    latest[0] = name

                def product(t, k):
                    for x, (wt, at_) in enumerate(((wH, aH), (wH, aL), (wL, aH))):
                        st = part == 0 and k == 0 and x == 0
                        en = final and k == nk - 1 and x == 2
                        if t[0] == "cm":
                            last = mm(ps[:, t[1], 0:T], wt[:, slot, k, t[2]:t[2] + P], at_[:, k0 + k, :],
                                      start=st, stop=en)
                        else:
                            last = mm(ps[:, t[1], 0:t[3]], at_[:, k0 + k, t[4] * P:(t[4] + 1) * P],
                                      wt[:, slot, k, t[2]:t[2] + t[3]], start=st, stop=en)
                    return last

                if part == 0 and name in FIRST_USE:
                    for m, t in enumerate(g["tiles"]):
                        if (name, m) in BANKFREE:
                            pe.wait_ge(*BANKFREE[name, m])
                    for k in range(nk):
                        pe.wait_ge(*operand_ready(name, k))
                        for t in g["tiles"]:
                            last = product(t, k)
                else:
                    for m, t in enumerate(g["tiles"]):
                        if part == 0 and (name, m) in BANKFREE:
                            pe.wait_ge(*BANKFREE[name, m])
                        for k in range(nk):
                            if m == 0 and name in FIRST_USE:
                                pe.wait_ge(*operand_ready(name, k0 + k))
                            last = product(t, k)
                        if final:
                            last.then_inc(on.tile_done, 1)
                if not final:
                    last.then_inc(on.panel_done, 1)

            pe.wait_ge(on.pool_step, 5)
            for e in TL:
                k = e[0]
                if k == "load_x":
                    for b in range(4):
                        pe.wait_ge(on.in_x[b], 16)
                        for kk in range(2):
                            for j in range(TB):
                                last = tr(ps[:, 4 + b, kk * T + j * P:kk * T + (j + 1) * P],
                                          xtok[:, j, (2 * b + kk) * P:(2 * b + kk + 1) * P])
                        last.then_inc(on.x_psum, 1)
                elif k == "panel":
                    panel(e[1], e[2])
                elif k == "norm":
                    n = e[1]
                    pe.wait_ge(on.ada_done, ada_sums[0])
                    if n == 0:
                        pe.wait_ge(on.x_done, KD)
                    for kk in range(KD):
                        pe.wait_ge(on.sq_done, 8 * n + kk + 1)
                        for j in range(TB):
                            last = mm(ss[:, j:j + 1], SQ[:, kk, j * P:(j + 1) * P], ones[:, 0:1], start=kk == 0,
                                      stop=kk == KD - 1)
                        if n == 2:
                            pe.wait_ge(on.sq2_done, kk + 1)
                            for j in range(TB):
                                last = mm(ss2[:, j:j + 1], SQ2[:, kk, j * P:(j + 1) * P], ones[:, 0:1], start=kk == 0,
                                          stop=kk == KD - 1)
                    last.then_inc(on.ss_done, 1)
                    if n == 2:
                        pe.wait_ge(on.rd2_done, 1)
                        for j in range(TB):
                            spread(rb[:, j * P:(j + 1) * P], R2a[:, j:j + 1])
                        for j in range(TB):
                            last = spread(rb2[:, j * P:(j + 1) * P], R1[:, j:j + 1])
                    else:
                        pe.wait_ge(on.rd_done, n + 1)
                        for j in range(TB):
                            last = spread(rb[:, j * P:(j + 1) * P], R1[:, j:j + 1])
                    last.then_inc(on.bcast, 1)
                elif k == "ada_sum":
                    q = e[1]
                    pe.wait_ge(on.w_lo, SIDX["ada", 2 * q + 1] + 1)
                    pe.wait_ge(on.ada_done, q)
                    if q == 0:
                        pe.wait_ge(on.x_done, KD)
                    elif q == 2:
                        pe.wait_ge(on.o_sq, 4)
                    elif q == 7:
                        pe.wait_ge(on.tmp_done, 16)
                    for t in range(4):
                        last = mm(adaps[:, t:t + 1], acc[:, t * P:(t + 1) * P], ones[:, 0:1], start=True, stop=True)
                    last.then_inc(on.ada_psum, 1)
                    ada_sums[0] += 1
                elif k == "scores":
                    u = e[1]
                    kind, n, h0, nh, nk = UNITS[u]
                    if u:
                        pe.wait_ge(on.probs, u)
                    if u > 1:
                        pe.wait_ge(on.yT_done, u - 1)
                    if kind == 1:
                        pe.wait_ge(on.consts, 1)
                        pe.wait_ge(*EV["q1", 3])
                        pe.wait_ge(on.kz, 4)
                        pe.wait_ge(on.ada_done, 2)
                    else:
                        pe.wait_ge(*EV["q2", 3])
                        pe.wait_ge(*EV["k2", 3])
                        pe.wait_ge(on.in_R2, 16)
                        pe.wait_ge(on.seg, 2)
                    for hh in range(nh):
                        h = h0 + hh
                        o = sc45[:, hh * nk * P:(hh + 1) * nk * P]
                        ks = slice(0, nk * P) if n else slice(0, P)
                        if kind == 1:
                            mm(o, identb[:], mask1[:, (2 - nk) * P:2 * P], start=True, stop=False)
                            last = mm(o, aQ[:, h // 2, n * P:(n + 1) * P], aKZ[:, 2 * (h // 8) + h % 2, ks],
                                      start=False, stop=True)
                        else:
                            mm(o, J[:], R2[:, h, (2 - nk) * P:2 * P], start=True, stop=False)
                            mm(o[:, (nk - 1) * P:nk * P], identb[:], mask2[:], start=False, stop=False)
                            last = mm(o, q2[:, h // 2, n * P:(n + 1) * P], k2z[:, h, ks], start=False, stop=True)
                    last.then_inc(on.scores_done, 1)
                elif k == "pt":
                    u = e[1]
                    pe.wait_ge(on.probs, u + 1)
                    if u:
                        pe.wait_ge(on.pv_done, u)
                        pe.wait_ge(on.pt_done, u)
                    if u == NU1:
                        pe.wait_ge(on.sy, 4)
                        pe.wait_ge(on.cb, 2)
                    for b in range(8):
                        last = tr(pt67[:, b * P:(b + 1) * P], PR[:, b, :])
                    last.then_inc(on.pt_psum, 1)
                elif k == "pv":
                    u = e[1]
                    kind, n, h0, nh, nk = UNITS[u]
                    pe.wait_ge(on.pt_done, u + 1)
                    if kind == 1:
                        pe.wait_ge(*EV["kv", 2])
                    else:
                        pe.wait_ge(*EV["v2", 1])
                    for hh in range(nh):
                        h = h0 + hh
                        for kb in range(nk):
                            vv = aV[:, kb, (h // 8) * DH:(h // 8 + 1) * DH] if kind == 1 else v2[:, kb, h * DH:(h + 1) * DH]
                            last = mm(ps[:, 6, hh * DH:(hh + 1) * DH], PT[:, hh * nk + kb, :], vv, start=kb == 0,
                                      stop=kb == nk - 1)
                    last.then_inc(on.pv_psum, 1)
                elif k == "yT":
                    u = e[1]
                    kind, n, h0, nh, nk = UNITS[u]
                    pe.wait_ge(on.pv_done, u + 1)
                    nxt = u + 1 < len(UNITS) and UNITS[u + 1][0] == kind
                    pe.wait_ge(on.probs, u + 1 + nxt)
                    for b in range(nh // 2):
                        last = tr(ps[:, 4, b * P:(b + 1) * P], YT[:, b * P:(b + 1) * P])
                    last.then_inc(on.yT_psum, 1)
                elif k == "hA":
                    s = e[1]
                    pe.wait_ge(on.hKp, s + 1)
                    pe.wait_ge(on.hKk, s + 1)
                    if s == 0:
                        pe.wait_ge(on.yT_done, NU1)
                        pe.wait_ge(on.pv_done, NU1)
                        pe.wait_ge(on.probs, NU1)
                    else:
                        pe.wait_ge(on.o_sq, 2 * s)
                        pe.wait_ge(on.o_rt, s)
                    for j in range(TB):
                        for h in range(4):
                            for c in range(2):
                                t0 = j * P + c * C
                                last = mm(ps[C * c:C * c + C, 4, (4 * j + h) * C:(4 * j + h + 1) * C],
                                          hKp[:, h, t0:t0 + C], hQp[:, h, t0:t0 + C], start=True, stop=True)
                    last.then_inc(on.hat_psum, 1)
                    for j in range(TB):
                        for h in range(4):
                            last = tr(ps[:, 5 + j, h * P:(h + 1) * P], hK[:, h, j * P:(j + 1) * P])
                    last.then_inc(on.hkt_psum, 1)
                elif k == "hB":
                    s = e[1]
                    pe.wait_ge(*EV[f"hi{s}", 1])
                    pe.wait_ge(on.hkt, 2 * s + 2)
                    for c in range(3):
                        r = slice(C * (c % 2), C * (c % 2) + C)
                        for h in range(4):
                            cs = slice(h * P, h * P + P)
                            last = mm(ps[:, (7, 5, 6)[c], cs], hKT[r, c // 2, cs], hV[r, c // 2, cs], start=True,
                                      stop=True)
                        last.then_inc(on.hkv_psum, 1)
                elif k == "hC":
                    s = e[1]
                    pe.wait_ge(on.hat, 2 * s + 2)
                    pe.wait_ge(on.hS, 9 * s + 9)
                    pe.wait_ge(on.hQq, s + 1)
                    for j in range(TB):
                        for h in range(4):
                            o = ps[:, 4 + 3 * j, h * P:(h + 1) * P]
                            cs = slice(h * P, h * P + P)
                            mm(o, hV[:, j, cs], hAT[:, 4 * j + h, :], start=True, stop=False)
                            for c in range(2):
                                if 2 * j + c:
                                    last = mm(o[:, c * C:(c + 1) * C], hS[:, 2 * j + c - 1, cs],
                                              hQ[:, h, j * P + c * C:j * P + (c + 1) * C], start=False, stop=c == 1)
                        last.then_inc(on.o_psum, 1)
                elif k == "hD":
                    s = e[1]
                    pe.wait_ge(on.o_sq, 2 * s + 2)
                    for h in range(4):
                        for j in range(TB):
                            last = mm(ps[:, 5, 2 * h + j:2 * h + j + 1], T2[:, h, j * P:(j + 1) * P], ones[:, 0:1],
                                      start=True, stop=True)
                    last.then_inc(on.oss_psum, 1)
                    pe.wait_ge(on.o_rd, s + 1)
                    for x in range(8):
                        last = spread(ps[:, 5 + x // 4, (x % 4) * P:(x % 4 + 1) * P], oR1[:, x:x + 1])
                    last.then_inc(on.o_bcast, 1)
                elif k == "dt":
                    pe.wait_ge(on.dtw_lo, 1)
                    for j in range(TB):
                        for kk in range(KD):
                            pe.wait_ge(on.u_ready, 16 + kk + 1)
                            js = slice(j * P, (j + 1) * P)
                            for x, (wt, at_) in enumerate(((dtH, p1H), (dtH, p1L), (dtL, p1H))):
                                last = mm(ps[:, 7, j * 8:(j + 1) * 8], at_[:, kk, js], wt[:, kk, :],
                                          start=kk == 0 and x == 0, stop=kk == KD - 1 and x == 2)
                    last.then_inc(on.dt_psum, 1)
                elif k == "xdt":
                    pe.wait_ge(on.xc_done, 1)
                    pe.wait_ge(on.adt, 1)
                    for j in range(TB):
                        for t in range(4):
                            last = tr(ps[:, 6 + j, t * P:(t + 1) * P], XC[:, t, j * P:(j + 1) * P])
                        last.then_inc(on.xd_psum, 1)
                elif k == "sA":
                    g = e[1]
                    pe.wait_ge(on.adt, 1)
                    if g:
                        pe.wait_ge(on.seg, g)
                        pe.wait_ge(on.cb, g)
                    a = sc45.rearrange("p (h n) -> p h n", h=4)
                    for h in range(4):
                        for j in range(TB):
                            last = mm(a[:, h, j * P:(j + 1) * P], ADT[:, j, 4 * g + h:4 * g + h + 1].broadcast_to([P, P]),
                                      CL[:], start=True, stop=True)
                    last.then_inc(on.abc_psum, 1)
                    pe.wait_ge(on.xd, 2)
                    if g == 0:
                        for x, terms in enumerate((((M0, 0),), ((M1, 0),), ((SL, 0),), ((SL, 0), (OL, 1)),
                                                   ((M0, 1),), ((M1, 1),))):
                            for y, (mat, j) in enumerate(terms):
                                last = mm(ps[:, 7, 64 + 8 * x:72 + 8 * x], mat[:], ADT[:, j, :], start=y == 0,
                                          stop=y == len(terms) - 1)
                        last.then_inc(on.bm_psum, 1)
                    pe.wait_ge(on.xc_done, 2)
                    mm(ps[:, 6, 0:T], XC[:, 4 + g, 0:P], XC[:, 6 + g, :], start=True, stop=True)
                    last = mm(ps[:, 6, T:T + P], XC[:, 4 + g, P:T], XC[:, 6 + g, P:T], start=True, stop=True)
                    last.then_inc(on.cb_psum, 1)
                elif k == "sY":
                    g = e[1]
                    pe.wait_ge(on.g_done, g + 1)
                    if g:
                        pe.wait_ge(on.sy, 2 * g)
                    for hh in range(4):
                        h = 4 * g + hh
                        o = ps[C * (hh % 2):C * (hh % 2) + C, 7, (hh // 2) * T:(hh // 2 + 1) * T]
                        mm(o, XD[:, 0, h * DH:(h + 1) * DH], SG[:, hh, 0:T], start=True, stop=False)
                        last = mm(o[:, P:T], XD[:, 1, h * DH:(h + 1) * DH], SG[:, hh, T:T + P], start=False, stop=True)
                    last.then_inc(on.sy_psum, 1)
                elif k == "snorm":
                    pe.wait_ge(on.ysq, 1)
                    banks_read()
                    for t in range(4):
                        for j in range(TB):
                            last = mm(yss[:, j:j + 1], sT[:, t, j * P:(j + 1) * P], ones[:, 0:1], start=t == 0,
                                      stop=t == 3)
                    last.then_inc(on.yss, 1)
                    pe.wait_ge(on.yrd, 1)
                    for j in range(TB):
                        last = spread(yrb[:, j * P:(j + 1) * P], R1[:, j:j + 1])
                    last.then_inc(on.ybcast, 1)
                elif k == "store":
                    pe.wait_ge(on.ot_done, 8)
                    for j in range(TB):
                        for kk in range(KD):
                            last = tr(ps[:, 4 + 2 * j + kk // 4, (kk % 4) * P:(kk % 4 + 1) * P],
                                      OT[:, kk, j * P:(j + 1) * P])
                            if kk % 4 == 3:
                                last.then_inc(on.ot_psum, 1)


INPUTS = ["x", "w_in", "b_in", "w_branch_attn", "w_branch_hgrn", "w_out", "w_ffn_gate", "w_ffn_up", "w_ffn_down",
          "w_ada_2", "w_in_2", "w_out_2", "w_up_2", "w_down_2"]


def kernel(**inputs):
    import numpy as np
    import concourse.bacc as bacc
    from concourse.bass_utils import run_bass_kernel_spmd

    def cols(a):
        return np.asarray(a).reshape(-1, P).T

    def rows(a):
        return np.broadcast_to(np.asarray(a).reshape(1, -1), (P, np.asarray(a).size))

    lb = np.asarray(inputs["hgrn_lb_logits"])
    params = np.concatenate([
        cols(inputs["norm_mix_g"]), cols(inputs["b_in"]), cols(lb[0]), cols(lb[1]), cols(inputs["hgrn_norm_g"]),
        cols(inputs["norm_ffn_g"]), cols(inputs["norm_final_g"]), cols(inputs["c_2"]), cols(inputs["norm_mix_w_2"]),
        cols(inputs["b_ada_2"]), cols(inputs["ssd_conv_w_2"]), cols(inputs["ssd_conv_b_2"]),
        cols(np.repeat(np.asarray(inputs["d_skip_2"]).reshape(-1), 64)), cols(inputs["ssd_norm_w_2"]),
        cols(inputs["norm_ffn_w_2"]), cols(inputs["ffn_conv_w_2"]), cols(inputs["final_norm_w_2"]),
        rows(inputs["attn_sinks"]), rows(inputs["dt_bias_2"]), rows(inputs["a_log_2"])], axis=1)
    nc = bacc.Bacc("TRN2", target_bir_lowering=False, num_devices=1)
    given = {name: np.ascontiguousarray(inputs[name]) for name in INPUTS}
    given["params"] = np.ascontiguousarray(params)
    given["rel_rev"] = np.ascontiguousarray(np.asarray(inputs["rel_bias_2"])[0, :, ::-1])
    arrays, IN = {}, {}
    for name, a in given.items():
        arrays["in_" + name] = a
        IN[name] = nc.dram_tensor("in_" + name, a.shape, mybir.dt.from_np(a.dtype), kind="ExternalInput").ap()
    out = nc.dram_tensor("out", (1, T, D), F32, kind="ExternalOutput").ap()
    build(nc, IN, out)
    return run_bass_kernel_spmd(nc, [arrays], core_ids=[0]).results[0]["out"]
```

```python
from contextlib import ExitStack

import concourse.bass as bass
from concourse import mybir

F32 = mybir.dt.float32
F32R = mybir.dt.float32r
BF16 = mybir.dt.bfloat16
U32 = mybir.dt.uint32
ACT = mybir.ActivationFunctionType
ALU = mybir.AluOpType
AX_X = mybir.AxisListType.X

P = 128
D = 1024
KD = D // P
T = 256
TB = T // P
DH = 64
C = 64
FF = 2816
KF = FF // P
EPS = 1e-6
NEG = -1e30
NRAW, NHL = 4, 3
AHEAD = NHL - 1
KP = 4
W = 512

PAR = {}
NPAR = 0
for _name, _n in (("norm_mix_g", 8), ("b_in", 58), ("lb0", 8), ("lb1", 8), ("hgrn_norm_g", 8),
                  ("norm_ffn_g", 8), ("norm_final_g", 8), ("c", 8), ("norm_mix_w_2", 8), ("b_ada", 48),
                  ("conv_w", 32), ("conv_b", 8), ("d_skip", 4), ("ssd_norm_w", 4), ("norm_ffn_w_2", 8),
                  ("ffn_conv_w", 132), ("final_norm_w", 8), ("sinks", 16), ("dt_bias", 8), ("a_log", 8)):
    PAR[_name] = (NPAR, _n)
    NPAR += _n


def cm_tiles(bank=0):
    return [("cm", bank + m, m * P) for m in range(4)]


def tm_tiles(off, width):
    return [("tm", 2 + j, off, width, j) for j in range(TB)]


def group(weights, segments, tiles, evac, operand, kblocks=KD, kbase=0):
    parts = [(k, min(KP, kblocks - k)) for k in range(0, kblocks, KP)]
    return dict(w=weights, seg=segments, tiles=tiles, evac=evac, act=operand, parts=parts, kbase=kbase)


GROUPS = {}
for _i in range(2):
    for _name, _c in (("q", 0), ("hq", 1280), ("hf", 2304), ("hg", 4352), ("ga", 5376), ("gb", 6400)):
        GROUPS[f"{_name}{_i}"] = group("w_in", [(_c + _i * W, W)], cm_tiles(), "AAAA", "P1")
    GROUPS[f"hi{_i}"] = group("w_in", [(3328 + _i * W, W)], tm_tiles(0, W), "DD", "P1")
    GROUPS[f"ba{_i}"] = group("w_branch_attn", [(_i * W, W)], cm_tiles(), "DDDD", "PY")
    GROUPS[f"bh{_i}"] = group("w_branch_hgrn", [(_i * W, W)], cm_tiles(), "DDDD", "PY")
    GROUPS[f"out{_i}"] = group("w_out", [(_i * W, W)], cm_tiles(4 - 4 * _i), "DDDD", "P1")
    GROUPS[f"down{_i}"] = group("w_ffn_down", [(_i * W, W)], cm_tiles(), "DDDD", "Z", KF)
    GROUPS[f"oo{_i}"] = group("w_out_2", [(_i * W, W)], cm_tiles(), "DDDD", "PY")
    GROUPS[f"dd{_i}"] = group("w_down_2", [(_i * W, W)], cm_tiles(4 - 4 * _i), "DDDD", "Z", KF)
GROUPS["kv"] = group("w_in", [(1024, 256)], [("cm", 0, 0)] + tm_tiles(128, 128), "ADD", "P1")
NF = FF // 256
for _i in range(NF):
    GROUPS[f"f{_i}"] = group(("w_ffn_gate", "w_ffn_up"), [(_i * 256, 256), (_i * 256, 256)], cm_tiles(), "AADD", "P1")
    GROUPS[f"u{_i}"] = group("w_up_2", [(_i * 256, 256), (FF + _i * 256, 256)], cm_tiles(_i % 2 * 4), "AAAA", "P1")
for _name, _c in (("z", 0), ("xs", 512), ("bc", 1024), ("q2", 1544), ("k2", 2056)):
    GROUPS[_name] = group("w_in_2", [(_c, W)], cm_tiles(), "AAAA", "P1")
GROUPS["v2"] = group("w_in_2", [(2568, W)], tm_tiles(0, W), "DD", "P1")

UNITS = [(1, 0, 0, 8, 1), (1, 0, 8, 8, 1), (1, 1, 0, 4, 2), (1, 1, 4, 4, 2), (1, 1, 8, 4, 2), (1, 1, 12, 4, 2),
         (2, 0, 0, 8, 1), (2, 1, 0, 4, 2), (2, 1, 4, 4, 2)]
NU1 = 6


WITH_ADA = [(_n, 1) for _n in ("q0", "q1")] + [("ga1", 0)]
WITH_ADA += [(_n, 0) for _n in ("out0", "out1")] + [(f"f{_i}", 0) for _i in range(NF)]
WITH_ADA += [(_n, _i) for _n in ("down0", "down1") for _i in range(4)]


class Signals:
    pass


def timeline():
    tl = [("load_x",), ("norm", 0), ("vectors",)]
    ada = iter(range(24))
    later = []

    def gemm(name, *after):
        parts = len(GROUPS[name]["parts"])
        for i in range(parts):
            tl.append(("panel", name, i))
            tl.extend(later)
            later.clear()
            if (name, i) in WITH_ADA:
                j = next(ada)
                tl.append(("ada", j))
                if j % 2:
                    later.append(("ada_sum", j // 2))
            if i == parts - 1:
                tl.append(("evac", name))
                if name.rstrip("0123456789") in ("f", "u", "xs", "bc", "hf"):
                    later.append(("tail", name))
            if i < len(after):
                tl.extend(after[i])

    def X(u):
        return [("pv", u - 1)] * (u > 0) + [("scores", u)] * (u < NU1)

    def Y(u):
        return [("pt", u)] * (u < NU1) + [("yT", u - 1)] * (u > 0)

    gemm("q0", [], [("setup",)])
    gemm("q1")
    gemm("kv", [], X(0))
    gemm("ga0", Y(0), X(1))
    gemm("ga1", Y(1), X(2))
    gemm("hq0", Y(2), X(3))
    gemm("hf0", Y(3), X(4))
    gemm("hi0", Y(4), X(5) + [("hprep", 0, 0)])
    gemm("hg0", Y(5) + [("hprep", 0, 1)], X(6) + [("hprep", 0, 2)])
    gemm("gb0", Y(6) + [("hprep", 0, 3)], [])
    gemm("gb1", [("hA", 0)], [("hB", 0)])
    gemm("hq1", [("hC", 0), ("hD", 0)])
    gemm("hf1")
    gemm("hi1", [("hprep", 1, 0), ("hprep", 1, 1)], [("hprep", 1, 2)])
    gemm("hg1", [("hprep", 1, 3)])
    gemm("ba0", [("hA", 1)], [("hB", 1)])
    gemm("ba1", [("hC", 1)], [("hsplit", 0), ("hD", 1), ("hsplit", 1)])
    gemm("bh0")
    gemm("bh1", [("merge", 0)], [("merge", 1)])
    gemm("out0")
    gemm("out1", [("squares", 1)], [("norm", 1)])
    for i in range(NF):
        gemm(f"f{i}")
    gemm("down0")
    gemm("down1", [], [], [("squares", 2)], [("first_sums",)], [("mod",)], [("norm", 2)])
    assert next(ada, None) is None, "every panel of w_ada has its place"
    gemm("xs", [("h_final",)])
    gemm("bc", [("dt",)])
    gemm("q2", [], [("xdt",), ("sA", 0)])
    gemm("k2", [("sY", 0), ("sA", 1)], [("sY", 1), ("scores", 6)])
    gemm("v2", [("pt", 6)], [("pv", 6), ("scores", 7)])
    gemm("z", [("pt", 7), ("yT", 6)], [("pv", 7), ("ysum",), ("snorm",), ("scores", 8)])
    gemm("oo0", [("pt", 8), ("yT", 7), ("pv", 8), ("yT", 8)])
    gemm("oo1", [("squares", 3)], [("norm", 3)])
    for i in range(NF):
        gemm(f"u{i}")
    gemm("dd0")
    gemm("dd1", [("gain",)], [("turn",)], [("squares", 4)], [], [], [("norm", 4), ("store",)])
    return tl


def build(nc, IN, out):
    TL = timeline()
    panels = [(e[1], e[2]) for e in TL if e[0] == "panel"]
    PIDX = {p: i for i, p in enumerate(panels)}

    stream = [("w", q) for q in range(AHEAD)]
    for e in TL:
        if e[0] == "panel" and PIDX[e[1:]] + AHEAD < len(panels):
            stream.append(("w", PIDX[e[1:]] + AHEAD))
        elif e[0] == "ada":
            stream.append(("ada", e[1]))
    SIDX = {s: i for i, s in enumerate(stream)}
    slot_loads, landed = [0] * NRAW, []
    for i, (kind, q) in enumerate(stream):
        slot_loads[i % NRAW] += 16 * (len(GROUPS[panels[q][0]]["seg"]) if kind == "w" else 1)
        landed.append(slot_loads[i % NRAW])

    with ExitStack() as ctx:
        on = Signals()
        on.a_exp = ctx.enter_context(nc.semaphore("a_exp"))
        on.abc_psum = ctx.enter_context(nc.semaphore("abc_psum"))
        on.ada_done = ctx.enter_context(nc.semaphore("ada_done"))
        on.ada_psum = ctx.enter_context(nc.semaphore("ada_psum"))
        on.adt = ctx.enter_context(nc.semaphore("adt"))
        on.bcast = ctx.enter_context(nc.semaphore("bcast"))
        on.bm_psum = ctx.enter_context(nc.semaphore("bm_psum"))
        on.cb = ctx.enter_context(nc.semaphore("cb"))
        on.cb_psum = ctx.enter_context(nc.semaphore("cb_psum"))
        on.consts = ctx.enter_context(nc.semaphore("consts"))
        on.conv0 = ctx.enter_context(nc.semaphore("conv0"))
        on.conv_done = ctx.enter_context(nc.semaphore("conv_done"))
        on.dsink = ctx.enter_context(nc.semaphore("dsink"))
        on.dt_abs = ctx.enter_context(nc.semaphore("dt_abs"))
        on.dt_e = ctx.enter_context(nc.semaphore("dt_e"))
        on.dt_ln = ctx.enter_context(nc.semaphore("dt_ln"))
        on.dt_psum = ctx.enter_context(nc.semaphore("dt_psum"))
        on.dtw_hi = ctx.enter_context(nc.semaphore("dtw_hi"))
        on.dtw_lo = ctx.enter_context(nc.semaphore("dtw_lo"))
        on.dve_step = ctx.enter_context(nc.semaphore("dve_step"))
        on.esink = ctx.enter_context(nc.semaphore("esink"))
        on.evac_act = ctx.enter_context(nc.semaphore("evac_act"))
        on.evac_dve = ctx.enter_context(nc.semaphore("evac_dve"))
        on.ext_done = ctx.enter_context(nc.semaphore("ext_done"))
        on.ext_out = ctx.enter_context(nc.semaphore("ext_out"))
        on.g_done = ctx.enter_context(nc.semaphore("g_done"))
        on.hE1 = ctx.enter_context(nc.semaphore("hE1"))
        on.hE2 = ctx.enter_context(nc.semaphore("hE2"))
        on.hE3 = ctx.enter_context(nc.semaphore("hE3"))
        on.hE4 = ctx.enter_context(nc.semaphore("hE4"))
        on.hE5 = ctx.enter_context(nc.semaphore("hE5"))
        on.hKk = ctx.enter_context(nc.semaphore("hKk"))
        on.hKp = ctx.enter_context(nc.semaphore("hKp"))
        on.hQp = ctx.enter_context(nc.semaphore("hQp"))
        on.hQq = ctx.enter_context(nc.semaphore("hQq"))
        on.hS = ctx.enter_context(nc.semaphore("hS"))
        on.h_final = ctx.enter_context(nc.semaphore("h_final"))
        on.hat = ctx.enter_context(nc.semaphore("hat"))
        on.hat_psum = ctx.enter_context(nc.semaphore("hat_psum"))
        on.hb_done = ctx.enter_context(nc.semaphore("hb_done"))
        on.hdl = ctx.enter_context(nc.semaphore("hdl"))
        on.hdm = ctx.enter_context(nc.semaphore("hdm"))
        on.hf_log = ctx.enter_context(nc.semaphore("hf_log"))
        on.hfin = ctx.enter_context(nc.semaphore("hfin"))
        on.hk_done = ctx.enter_context(nc.semaphore("hk_done"))
        on.hkt = ctx.enter_context(nc.semaphore("hkt"))
        on.hkt_psum = ctx.enter_context(nc.semaphore("hkt_psum"))
        on.hkv_psum = ctx.enter_context(nc.semaphore("hkv_psum"))
        on.hq_done = ctx.enter_context(nc.semaphore("hq_done"))
        on.hs_done = ctx.enter_context(nc.semaphore("hs_done"))
        on.hsh = ctx.enter_context(nc.semaphore("hsh"))
        on.in_R2 = ctx.enter_context(nc.semaphore("in_R2"))
        on.in_brow = ctx.enter_context(nc.semaphore("in_brow"))
        on.in_dtw = ctx.enter_context(nc.semaphore("in_dtw"))
        on.in_par = ctx.enter_context(nc.semaphore("in_par"))
        on.in_rel = ctx.enter_context(nc.semaphore("in_rel"))
        on.in_x = [ctx.enter_context(nc.semaphore(f"in_x{b}")) for b in range(4)]
        on.k2_half = ctx.enter_context(nc.semaphore("k2_half"))
        on.kz = ctx.enter_context(nc.semaphore("kz"))
        on.kz_zero = ctx.enter_context(nc.semaphore("kz_zero"))
        on.lb_diff = ctx.enter_context(nc.semaphore("lb_diff"))
        on.lb_sig = ctx.enter_context(nc.semaphore("lb_sig"))
        on.c_silu = ctx.enter_context(nc.semaphore("c_silu"))
        on.merged = ctx.enter_context(nc.semaphore("merged"))
        on.mh = ctx.enter_context(nc.semaphore("mh"))
        on.mixed = ctx.enter_context(nc.semaphore("mixed"))
        on.negb = ctx.enter_context(nc.semaphore("negb"))
        on.negmax = ctx.enter_context(nc.semaphore("negmax"))
        on.o_bcast = ctx.enter_context(nc.semaphore("o_bcast"))
        on.o_copy = ctx.enter_context(nc.semaphore("o_copy"))
        on.o_psum = ctx.enter_context(nc.semaphore("o_psum"))
        on.o_rt = ctx.enter_context(nc.semaphore("o_rt"))
        on.o_rd = ctx.enter_context(nc.semaphore("o_rd"))
        on.o_sq = ctx.enter_context(nc.semaphore("o_sq"))
        on.oss_psum = ctx.enter_context(nc.semaphore("oss_psum"))
        on.ot_done = ctx.enter_context(nc.semaphore("ot_done"))
        on.ot_psum = ctx.enter_context(nc.semaphore("ot_psum"))
        on.out_left = ctx.enter_context(nc.semaphore("out_left"))
        on.out_right = ctx.enter_context(nc.semaphore("out_right"))
        on.panel_done = ctx.enter_context(nc.semaphore("panel_done"))
        on.pool_step = ctx.enter_context(nc.semaphore("pool_step"))
        on.probs = ctx.enter_context(nc.semaphore("probs"))
        on.probs_part = ctx.enter_context(nc.semaphore("probs_part"))
        on.pt_done = ctx.enter_context(nc.semaphore("pt_done"))
        on.pt_part = ctx.enter_context(nc.semaphore("pt_part"))
        on.pt_psum = ctx.enter_context(nc.semaphore("pt_psum"))
        on.pv_done = ctx.enter_context(nc.semaphore("pv_done"))
        on.pv_psum = ctx.enter_context(nc.semaphore("pv_psum"))
        on.act_fetch = ctx.enter_context(nc.semaphore("act_fetch"))
        on.ms2_done = ctx.enter_context(nc.semaphore("ms2_done"))
        on.rt2_done = ctx.enter_context(nc.semaphore("rt2_done"))
        on.rd2_done = ctx.enter_context(nc.semaphore("rd2_done"))
        on.rt_done = ctx.enter_context(nc.semaphore("rt_done"))
        on.rd_done = ctx.enter_context(nc.semaphore("rd_done"))
        on.scores_done = ctx.enter_context(nc.semaphore("scores_done"))
        on.seg = ctx.enter_context(nc.semaphore("seg"))
        on.seg_exp = ctx.enter_context(nc.semaphore("seg_exp"))
        on.sig_part = ctx.enter_context(nc.semaphore("sig_part"))
        on.snh = ctx.enter_context(nc.semaphore("snh"))
        on.snorm_done = ctx.enter_context(nc.semaphore("snorm_done"))
        on.bcast2 = ctx.enter_context(nc.semaphore("bcast2"))
        on.gains2 = ctx.enter_context(nc.semaphore("gains2"))
        on.akz_zero = ctx.enter_context(nc.semaphore("akz_zero"))
        on.hat_zero = ctx.enter_context(nc.semaphore("hat_zero"))
        on.sq_sum = ctx.enter_context(nc.semaphore("sq_sum"))
        on.sq_done = ctx.enter_context(nc.semaphore("sq_done"))
        on.ss_done = ctx.enter_context(nc.semaphore("ss_done"))
        on.stored = ctx.enter_context(nc.semaphore("stored"))
        on.sy = ctx.enter_context(nc.semaphore("sy"))
        on.sy_psum = ctx.enter_context(nc.semaphore("sy_psum"))
        on.tile_done = ctx.enter_context(nc.semaphore("tile_done"))
        on.tmp_done = ctx.enter_context(nc.semaphore("tmp_done"))
        on.u_ready = ctx.enter_context(nc.semaphore("u_ready"))
        on.u_silu = ctx.enter_context(nc.semaphore("u_silu"))
        on.uconv0 = ctx.enter_context(nc.semaphore("uconv0"))
        on.uconv_done = ctx.enter_context(nc.semaphore("uconv_done"))
        on.uh_done = ctx.enter_context(nc.semaphore("uh_done"))
        on.ur_zero = ctx.enter_context(nc.semaphore("ur_zero"))
        on.w_hi = ctx.enter_context(nc.semaphore("w_hi"))
        on.w_lo = ctx.enter_context(nc.semaphore("w_lo"))
        on.x_done = ctx.enter_context(nc.semaphore("x_done"))
        on.x_psum = ctx.enter_context(nc.semaphore("x_psum"))
        on.xc_done = ctx.enter_context(nc.semaphore("xc_done"))
        on.xd = ctx.enter_context(nc.semaphore("xd"))
        on.xd_psum = ctx.enter_context(nc.semaphore("xd_psum"))
        on.xr_zero = ctx.enter_context(nc.semaphore("xr_zero"))
        on.yT_done = ctx.enter_context(nc.semaphore("yT_done"))
        on.yT_psum = ctx.enter_context(nc.semaphore("yT_psum"))
        on.yTh = ctx.enter_context(nc.semaphore("yTh"))
        on.yrt = ctx.enter_context(nc.semaphore("yrt"))
        on.yrd = ctx.enter_context(nc.semaphore("yrd"))
        on.ybcast = ctx.enter_context(nc.semaphore("ybcast"))
        on.ysq = ctx.enter_context(nc.semaphore("ysq"))
        on.yss = ctx.enter_context(nc.semaphore("yss"))
        on.ytmp = ctx.enter_context(nc.semaphore("ytmp"))
        on.yz = ctx.enter_context(nc.semaphore("yz"))
        on.z_silu = ctx.enter_context(nc.semaphore("z_silu"))
        on.z_ready = ctx.enter_context(nc.semaphore("z_ready"))
        on.zh_done = ctx.enter_context(nc.semaphore("zh_done"))
        on.zt_done = ctx.enter_context(nc.semaphore("zt_done"))
        on.raw = [ctx.enter_context(nc.semaphore(f"raw{i}")) for i in range(NRAW)]

        TILE, USED, EV = {}, {}, {}
        tiles = plain = 0
        ev = {"A": 0, "D": 0}
        for name, part in panels:
            g = GROUPS[name]
            if part == len(g["parts"]) - 1:
                for m in range(len(g["tiles"])):
                    tiles += 1
                    TILE[name, m] = tiles
                    ev[g["evac"][m]] += 1
                    EV[name, m] = (on.evac_act if g["evac"][m] == "A" else on.evac_dve, ev[g["evac"][m]])
                USED[PIDX[name, part]] = (on.tile_done, tiles)
            else:
                plain += 1
                USED[PIDX[name, part]] = (on.panel_done, plain)
        BANKFREE, last = {}, {}
        for name, part in panels:
            if part == 0:
                for m, t in enumerate(GROUPS[name]["tiles"]):
                    if t[1] in last:
                        BANKFREE[name, m] = last[t[1]]
                for m, t in enumerate(GROUPS[name]["tiles"]):
                    last[t[1]] = EV[name, m]

        def sb(name, shape, dt=F32):
            return ctx.enter_context(nc.sbuf_tensor(name, shape, dt))

        raw = sb("raw", [P, NRAW, KP, W])
        wH = sb("wH", [P, NHL, KP, W], F32R)
        wL = sb("wL", [P, NHL, KP, W], F32R)
        p1H = sb("p1H", [P, KD, T], F32R)
        p1L = sb("p1L", [P, KD, T], F32R)
        hT = sb("hT", [P, KD, T])
        SCRK = 70
        arena = sb("arena", [P, (16 + SCRK) * 256])
        base = nc.sbuf_base - (16 + SCRK) * 1024

        def at(name, kb, shape, dt):
            return nc.alloc_sbuf_tensor_at(name, shape, dt, offset=base + kb * 1024)

        pyH = at("pyH", 0, [P, KD, T], F32R)
        pyL = at("pyL", 8, [P, KD, T], F32R)
        zH = at("zH", 0, [P, KF, T], F32R)
        zL = at("zL", 22, [P, KF, T], F32R)

        def scr(kb, *dims):
            n = 1
            for d in dims:
                n *= d
            v = arena[:, int((16 + kb) * 256):int((16 + kb) * 256) + n]
            if len(dims) == 1:
                return v
            names = "abc"[:len(dims)]
            return v.rearrange(f"p ({' '.join(names)}) -> p {' '.join(names)}", **dict(zip(names[1:], dims[1:])))

        xtok = scr(12, TB, D)
        vrow, dtw, ext = scr(10, P), scr(10.5, KD, 8), scr(40, 384)[0:8]
        SQ, TMP = scr(44, KD, T), scr(52, KD, T)
        aQ, aK, aKZ, aV = scr(0, KD, T), scr(8, T), scr(66, 4, T), scr(9, TB, P)
        PR, PT, YT = scr(12, 8, P), scr(16, 8, P), scr(20, 512)
        hQp, hKp, hAT, hKT, hS = scr(0, 4, T), scr(4, 4, T), scr(8, 8, P), scr(12, TB, 512), scr(16, 3, 512)
        GA, GB = scr(22, KD, T), scr(30, KD, T)
        hQ, hK, hB, T1, T2 = scr(38, 4, T), scr(42, 4, T), scr(46, 4, T), scr(50, 4, T), scr(54, 4, T)
        hV, hG = scr(58, TB, 512), scr(62, 4, T)
        YF0 = scr(66, 4, T)
        XC, XR = scr(0, 8, T), scr(8, 4, T + 3)
        SG, CB, XD = scr(22, 4, 384), scr(28, 384), scr(30, TB, 512)
        sY, sZ, sT = scr(34, 4, T), scr(38, 4, T), scr(42, 4, T)
        q2, k2z, v2, R2 = scr(46, 4, T), scr(50, 8, T), scr(58, TB, 512), scr(62, 8, T)
        TG, ZT = scr(60, 2, T), scr(62, 2, T)
        UR, UC = scr(30, 4, T + 2), scr(36, 4, T)
        OT, OUT = scr(28, KD, T), scr(8, TB, D)

        par = sb("par", [P, NPAR])
        ident, ones = sb("ident", [P, P]), sb("ones", [P, P])
        identb = sb("identb", [P, P], BF16)
        mask1, mask2 = sb("mask1", [P, 256], BF16), sb("mask2", [P, P], BF16)
        hmask = sb("hmask", [P, C], U32)
        CL, M0, M1, SL, OL, J = (sb(n, [P, P]) for n in ("CL", "M0", "M1", "SL", "OL", "J"))
        UT = sb("UT", [P, P], BF16)
        reset = sb("reset", [P, T], BF16)
        R0, R1, R2a, oR0, oR1 = (sb(n, [P, w]) for n, w in (("R0", TB), ("R1", TB), ("R2a", TB), ("oR0", 8), ("oR1", 8)))
        G12, S12 = sb("G12", [P, KD, 2]), sb("S12", [P, TB, 2])
        eps2 = sb("eps2", [P, 1])
        XS, XSS = sb("XS", [P, TB, 4]), sb("XSS", [P, TB])
        fetch, fetch2 = sb("fetch", [P, 1]), sb("fetch2", [P, 1])
        acc = sb("acc", [P, W])
        brow = sb("brow", [P, D])
        eps, negb = sb("eps", [P, 1]), sb("negb", [P, 58])
        lb, oml, lbd = (sb(n, [P, 8]) for n in ("lb", "oml", "lbd"))
        cact, mod = sb("cact", [P, 8]), sb("mod", [P, 48])
        am, af = sb("am", [P, 8]), sb("af", [P, 8])
        RM, NM, DS, ES, SU, RD = (sb(n, [P, 2, 8]) for n in ("RM", "NM", "DS", "ES", "SU", "RD"))
        E5 = sb("E5", [P, 4, 4])
        dtH, dtL = sb("dtH", [P, KD, 8], F32R), sb("dtL", [P, KD, 8], F32R)
        DT, DR, DA, DE, ADT = (sb(n, [P, TB, 8]) for n in ("DT", "DR", "DA", "DE", "ADT"))
        nega, Bs = sb("nega", [P, 8]), sb("Bs", [P, 6, 8])
        ext_dram = nc.dram_tensor("ext_dram", (8, 384), F32).ap()

        ps = ctx.enter_context(nc.psum_tensor("ps", [P, 8, 512], F32))
        ss = ps[:, 4:6, 0]
        ssf = ps[:, 0:2, 0]
        rb = ps[:, 6, 256:512]
        rb2 = ps[:, 7, 256:512]
        yss, yrb = ps[:, 6:8, 0], ps[:, 7, 256:512]
        adaps = ps[:, 7, 508:512]
        sc45 = ps[:, 4:6, :].rearrange("p b n -> p (b n)")
        pt67 = ps[:, 6:8, :].rearrange("p b n -> p (b n)")

        def pc(name, i=0, n=1):
            return par[:, PAR[name][0] + i:PAR[name][0] + i + n]

        FIRST_USE = ("q0", "ba0", "bh0", "out0", "f0", "down0", "xs", "oo0", "u0", "dd0")
        OPND = {"P1": (p1H, p1L), "PY": (pyH, pyL), "Z": (zH, zL)}

        def operand_ready(name, k):
            if name[:3] == "out":
                return on.merged, k + 1
            if name[:2] == "ba":
                return on.yT_done, NU1
            if name[:2] == "bh":
                return on.hs_done, k // 4 + 1
            if name[:2] == "oo":
                return (on.snorm_done, k + 1) if k < 4 else (on.yT_done, 9)
            if name[:4] == "down":
                return on.z_ready, k // 2 + 1
            if name[:2] == "dd":
                return on.z_ready, NF + k // 2 + 1
            return on.u_ready, 8 * ("q0", "f0", "xs", "u0").index(name) + k + 1

        def h_ready(n, k):
            if n == 0:
                return on.x_done, k + 1
            return EV[f"{('out', 'down', 'oo', 'dd')[n - 1]}{k // 4}", k % 4]

        block = ctx.enter_context(nc.Block())

        @block.sync
        def _(sp):
            for b in range(4):
                sp.dma_start(xtok[:, :, b * T:(b + 1) * T],
                             IN["x"][0].rearrange("(j p) n -> p j n", p=P)[:, :, b * T:(b + 1) * T]).then_inc(on.in_x[b], 16)
                if b == 0:
                    sp.dma_start(par[:], IN["params"]).then_inc(on.in_par, 16)
            for i, (kind, q) in enumerate(stream):
                if i >= NRAW:
                    sp.wait_ge(on.w_lo, i - NRAW + 1)
                if kind == "w":
                    name, part = panels[q]
                    g = GROUPS[name]
                    k0, nk = g["parts"][part]
                    off = 0
                    for s, (c0, w) in enumerate(g["seg"]):
                        src = IN[g["w"] if isinstance(g["w"], str) else g["w"][s]][0]
                        src = src.rearrange("(k p) n -> p k n", p=P)[:, k0:k0 + nk, c0:c0 + w]
                        sp.dma_start(raw[:, i % NRAW, 0:nk, off:off + w], src).then_inc(on.raw[i % NRAW], 16)
                        off += w
                else:
                    src = IN["w_ada_2"][0].rearrange("(k p) n -> p k n", p=P)
                    src = src[:, (q % 2) * KP:(q % 2 + 1) * KP, (q // 2) * W:(q // 2 + 1) * W]
                    sp.dma_start(raw[:, i % NRAW, :, :], src).then_inc(on.raw[i % NRAW], 16)
                if i == 2:
                    bi = IN["b_in"]
                    sp.dma_start(brow[:], bi[0:1, 3328:3328 + D].partition_broadcast(P)).then_inc(on.in_brow, 16)
                    sp.dma_start(vrow, bi[0:1, 1152:1152 + P].partition_broadcast(P)).then_inc(on.in_brow, 16)
                    sp.dma_start(dtw, IN["w_in_2"][0].rearrange("(k p) n -> p k n", p=P)[:, :, 1536:1544]).then_inc(on.in_dtw, 16)
                    sp.dma_start(ext[:, P - 1:P - 1 + 257], IN["rel_rev"]).then_inc(on.in_rel, 16)
                if i == 10:
                    sp.wait_ge(on.ext_done, 1)
                    sp.dma_start(ext_dram[:, :], ext).then_inc(on.ext_out, 16)
                if kind == "w" and panels[q] == ("bc", 1):
                    sp.wait_ge(on.ext_out, 16)
                    sp.wait_ge(on.u_ready, 24)
                    sp.dma_start(R2, bass.AP(ext_dram.tensor, 0, [[1, P], [384, 8], [1, T]])).then_inc(on.in_R2, 16)
            for j in range(TB):
                sp.wait_ge(on.out_left, j + 1)
                sp.wait_ge(on.out_right, j + 1)
                sp.dma_start(out[0, j * P:(j + 1) * P, :], OUT[:, j, :]).then_inc(on.stored, 16)
            sp.wait_ge(on.stored, 16 * TB)

        @block.gpsimd
        def _(pool):

            steps = [0]

            def step(ins):
                steps[0] += 1
                ins.then_inc(on.pool_step, 1)
                pool.wait_ge(on.pool_step, steps[0])

            def select(t, cond, fill, op=ALU.is_ge):
                base_, mult, stp = cond
                step(pool.affine_select(out=t, in_=t, compare_op=op, fill=fill, base=base_,
                                        pattern=[[stp, t.shape[-1]]], channel_multiplier=mult))

            step(pool.memset(eps[:], EPS))
            step(pool.memset(nega[:], 0.0))
            step(pool.memset(eps2[:], EPS * EPS))
            step(pool.memset(ident[:], 0.0))
            select(ident[:], (0, 1, -1), 1.0, ALU.not_equal)
            step(pool.memset(ones[:], 1.0))
            step(pool.memset(identb[:], 0.0))
            select(identb[:], (0, 1, -1), 1.0, ALU.not_equal)
            step(pool.memset(mask1[:], 0.0))
            select(mask1[:, 0:P], (-1, -1, 1), NEG)
            select(mask1[:, P:2 * P], (0, 1, -1), NEG)
            step(pool.memset(mask2[:], 0.0))
            step(pool.memset(mask2[0:C, C:P], NEG))
            step(pool.memset(reset[:], 1.0))
            step(pool.memset(reset[:, 0:T:C], 0.0))
            step(pool.memset(J[:], 0.0))
            select(J[:], (-(P - 1), 1, 1), 1.0, ALU.not_equal)
            step(pool.memset(UT[:], 1.0))
            select(UT[:], (0, -1, 1), 0.0)
            step(pool.tensor_copy(CL[:], UT[:]))
            step(pool.memset(CL[0:C, C:P], 0.0))
            step(pool.memset(SL[:], 1.0))
            select(SL[:], (-1, 1, -1), 0.0)
            step(pool.memset(OL[:], 0.0))
            step(pool.memset(OL[0:C, :], 1.0))
            step(pool.memset(M0[:], 0.0))
            step(pool.tensor_scalar(M0[:, 0:C], CL[:, 0:C], -1.0, None, ALU.mult))
            step(pool.memset(M1[:], 0.0))
            step(pool.tensor_scalar(M1[:, C:P], CL[:, C:P], -1.0, None, ALU.mult))
            step(pool.tensor_copy(M1[0:C, 0:C], SL[0:C, 0:C]))
            step(pool.tensor_copy(hmask[0:C, :], UT[0:C, 0:C]))
            step(pool.tensor_copy(hmask[C:P, :], UT[C:P, C:P]))
            pool.memset(fetch2[:], 0.0).then_inc(on.consts, 1)
            pool.memset(aKZ, 0.0).then_inc(on.akz_zero, 1)
            for e in TL:
                if e[0] == "hprep" and e[2] == 2:
                    pool.wait_ge(on.hE3, e[1] + 1)
                    pool.wait_ge(on.hQp, e[1] + 1)
                    pool.tensor_tensor(hQ, hQ, T2, ALU.mult).then_inc(on.hQq, 1)
                elif e[0] == "hprep" and e[2] == 3:
                    if e[1]:
                        pool.wait_ge(on.o_psum, 2 * e[1])
                    else:
                        pool.wait_ge(on.kz, 4)
                        pool.wait_ge(on.dtw_lo, 1)
                        pool.wait_ge(on.pv_psum, NU1)
                    pool.memset(hAT, 0.0).then_inc(on.hat_zero, 1)
                elif e[0] == "norm" and e[1] == 2:
                    pool.wait_ge(on.u_ready, 24)
                    pool.memset(k2z, 0.0).then_inc(on.kz_zero, 1)
                if e[0] == "squares" and e[1] != 2:
                    n = e[1]
                    for k in range(1, 4):
                        pool.wait_ge(on.sq_done, 8 * n + k + 1)
                        ins = pool.tensor_tensor(SQ[:, 0], SQ[:, 0], SQ[:, k], ALU.add)
                        if k < 3:
                            step(ins)
                    ins.then_inc(on.sq_sum, 1)

        @block.scalar
        def _(act):

            def split_hi(q):
                i = SIDX["w", q]
                nk = GROUPS[panels[q][0]]["parts"][panels[q][1]][1]
                wd = sum(w for _, w in GROUPS[panels[q][0]]["seg"])
                act.wait_ge(on.raw[i % NRAW], landed[i])
                if q >= NHL:
                    act.wait_ge(*USED[q - NHL])
                nc.scalar.activation(wH[:, q % NHL, 0:nk, 0:wd], raw[:, i % NRAW, 0:nk, 0:wd], ACT.Copy).then_inc(on.w_hi, 1)

            def square(n, k):
                act.wait_ge(*h_ready(n, k))
                nc.scalar.activation(SQ[:, k], hT[:, k], ACT.Square).then_inc(on.sq_done, 1)

            def norm(n):
                nc.scalar.activation(fetch[:], eps[:], ACT.Sqrt).then_inc(on.act_fetch, 1)
                for k in range(4, KD if n else 0):
                    square(n, k)
                if n == 0:
                    for b in range(4):
                        act.wait_ge(on.in_x[b], 16)
                        for j in range(TB):
                            nc.scalar.activation(SQ[:, 2 * b + j], xtok[:, j, b * T:(b + 1) * T], ACT.Square,
                                                 accum_out=XS[:, j, b:b + 1]).then_inc(on.sq_done, 1)
                act.wait_ge(on.ss_done, n + 1)
                if n == 2:
                    act.wait_ge(on.ms2_done, 1)
                    nc.scalar.activation(R2a[:], R2a[:], ACT.Sqrt, scale=1.0 / D, bias=eps2[:, 0:1]).then_inc(on.rt2_done, 1)
                sums = {0: XSS[:], 2: S12[:, :, 0], 4: ssf}.get(n, ss)
                nc.scalar.activation(R0[:], sums, ACT.Sqrt, scale=1.0 / D, bias=eps[:, 0:1]).then_inc(on.rt_done, 1)
                if n == 4:
                    return
                if n == 0:
                    split_hi(0)
                for k in range(KD):
                    act.wait_ge(on.tmp_done, 8 * n + k + 1)
                    if n < 2:
                        nc.scalar.activation(p1H[:, k], TMP[:, k], ACT.Copy).then_inc(on.uh_done, 1)
                    else:
                        o = (0 if n == 2 else 24) + k
                        nc.scalar.activation(p1H[:, k], TMP[:, k], ACT.Identity,
                                             bias=mod[:, o:o + 1]).then_inc(on.uh_done, 1)
                if n == 0:
                    split_hi(1)

            def evac(name):
                g = name.rstrip("0123456789")
                i = int(name[len(g):] or 0)

                def each(dst, f, **kw):
                    for m, t in enumerate(GROUPS[name]["tiles"]):
                        if GROUPS[name]["evac"][m] == "A":
                            act.wait_ge(on.tile_done, TILE[name, m])
                            bias = {a: b(m) if callable(b) else b for a, b in kw.items()}
                            nc.scalar.activation(dst(m), ps[:, t[1], 0:T], f, **bias).then_inc(on.evac_act, 1)

                if g == "q" and name in ("q0", "q1"):
                    each(lambda m: aQ[:, 4 * i + m], ACT.Identity, bias=lambda m: pc("b_in", 4 * i + m))
                elif name == "kv":
                    each(lambda m: aK, ACT.Identity, bias=lambda m: pc("b_in", 8))
                elif g in ("ga", "gb"):
                    b0, G = (42, GA) if g == "ga" else (50, GB)
                    each(lambda m: G[:, 4 * i + m], ACT.Sigmoid, bias=lambda m: pc("b_in", b0 + 4 * i + m))
                elif g == "hq":
                    act.wait_ge(on.ext_out, 16)
                    if i:
                        act.wait_ge(on.o_psum, 2 * i)
                        act.wait_ge(on.hfin, i)
                    for m in range(4):
                        act.wait_ge(on.tile_done, TILE[name, m])
                        nc.scalar.activation(T1[:, m], ps[:, m, 0:T], ACT.Sigmoid,
                                             bias=pc("b_in", 10 + 4 * i + m)).then_inc(on.sig_part, 1)
                        nc.scalar.activation(hQ[:, m], ps[:, m, 0:T], ACT.Identity,
                                             bias=pc("b_in", 10 + 4 * i + m)).then_inc(on.evac_act, 1)
                elif g == "hf":
                    act.wait_ge(on.hq_done, i + 1)
                    for m in range(4):
                        act.wait_ge(on.tile_done, TILE[name, m])
                        nc.scalar.activation(T1[:, m], ps[:, m, 0:T], ACT.Sigmoid,
                                             bias=pc("b_in", 18 + 4 * i + m)).then_inc(on.sig_part, 1)
                        nc.scalar.activation(T2[:, m], ps[:, m, 0:T], ACT.Sigmoid, scale=-1.0,
                                             bias=negb[:, 18 + 4 * i + m:19 + 4 * i + m]).then_inc(on.evac_act, 1)
                elif g == "hg":
                    if i:
                        act.wait_ge(on.hfin, i)
                    each(lambda m: hG[:, m], ACT.Sigmoid, bias=lambda m: pc("b_in", 34 + 4 * i + m))
                elif g == "f":
                    each(lambda m: TG[:, m], ACT.Silu)
                elif g in ("xs", "bc"):
                    if g == "bc":
                        act.wait_ge(on.conv_done, 12)
                    act.wait_ge(on.xr_zero, 1)
                    each(lambda m: XR[:, m, 3:T + 3], ACT.Copy)
                    act.wait_ge(on.evac_act, EV[name, 3][1])
                    s = int(g == "bc")
                    for m in range(4):
                        nc.scalar.activation(XC[:, 4 * s + m], XR[:, m, 0:T], ACT.Identity, scale=pc("conv_w", 4 * s + m), bias=pc("conv_b", 4 * s + m)).then_inc(on.conv0, 1)
                elif name == "q2":
                    each(lambda m: q2[:, m], ACT.Copy, scale=0.125)
                elif name == "k2":
                    act.wait_ge(on.kz_zero, 1)
                    for m in range(4):
                        act.wait_ge(on.tile_done, TILE[name, m])
                        nc.scalar.activation(k2z[0:C, 2 * m], ps[0:C, m, 0:T], ACT.Copy).then_inc(on.k2_half, 1)
                        nc.scalar.activation(k2z[C:P, 2 * m + 1], ps[C:P, m, 0:T], ACT.Copy).then_inc(on.evac_act, 1)
                elif name == "z":
                    each(lambda m: sZ[:, m], ACT.Silu)
                elif g == "u":
                    act.wait_ge(on.ur_zero, 1)
                    if i:
                        act.wait_ge(on.uconv_done, 8 * i)
                    each(lambda m: UR[:, m, 2:T + 2], ACT.Copy)
                    act.wait_ge(on.evac_act, EV[name, 3][1])
                    for m in range(4):
                        wi = 2 * i + m % 2 + (KF if m > 1 else 0)
                        nc.scalar.activation(UC[:, m], UR[:, m, 0:T], ACT.Identity, scale=pc("ffn_conv_w", wi)).then_inc(on.uconv0, 1)

            def tail(name):
                g = name.rstrip("0123456789")
                i = int(name[len(g):] or 0)
                if g == "hf":
                    act.wait_ge(on.evac_act, EV[name, 3][1])
                    act.wait_ge(on.lb_sig, 2)
                    for h in range(4):
                        nc.scalar.activation(hB[:, h], T1[:, h], ACT.Ln, scale=oml[:, 4 * i + h:4 * i + h + 1],
                                             bias=lb[:, 4 * i + h:4 * i + h + 1]).then_inc(on.hf_log, 1)
                elif g in ("xs", "bc"):
                    s = int(g == "bc")
                    act.wait_ge(on.conv_done, 12 * s + 12)
                    nc.scalar.activation(XC[:, 4 * s:4 * s + 4], XC[:, 4 * s:4 * s + 4], ACT.Silu).then_inc(on.xc_done, 1)
                elif g == "f":
                    act.wait_ge(on.evac_dve, EV[name, 3][1])
                    nc.scalar.activation(zH[:, 2 * i:2 * i + 2], ZT, ACT.Copy).then_inc(on.zh_done, 1)
                else:
                    act.wait_ge(on.uconv_done, 8 * i + 8)
                    nc.scalar.activation(UC[:, 0:2], UC[:, 0:2], ACT.Silu).then_inc(on.u_silu, 1)
                    act.wait_ge(on.zt_done, i + 1)
                    nc.scalar.activation(zH[:, 2 * i:2 * i + 2], ZT, ACT.Copy).then_inc(on.zh_done, 1)

            act.wait_ge(on.pool_step, 3)
            for e in TL:
                k = e[0]
                if k == "vectors":
                    act.wait_ge(on.in_par, 16)
                    nc.scalar.activation(cact[:], pc("c", 0, 8), ACT.Silu).then_inc(on.c_silu, 1)
                    act.wait_ge(on.lb_diff, 1)
                    nc.scalar.activation(oml[:], lbd[:], ACT.Sigmoid, scale=-1.0).then_inc(on.lb_sig, 1)
                    nc.scalar.activation(lb[:], lbd[:], ACT.Sigmoid).then_inc(on.lb_sig, 1)
                    nc.scalar.activation(nega[:], pc("a_log", 0, 8), ACT.Exp).then_inc(on.a_exp, 1)
                if k == "panel":
                    q = PIDX[e[1:]] + AHEAD
                    if q < len(panels):
                        split_hi(q)
                elif k == "squares":
                    for kk in range(4):
                        square(e[1], kk)
                elif k == "norm":
                    norm(e[1])
                elif k == "evac":
                    evac(e[1])
                elif k == "tail":
                    tail(e[1])
                elif k == "setup":
                    act.wait_ge(on.in_dtw, 16)
                    nc.scalar.activation(dtH[:], dtw, ACT.Copy).then_inc(on.dtw_hi, 1)
                elif k == "scores":
                    u = e[1]
                    kind, n, h0, nh, nk = UNITS[u]
                    act.wait_ge(on.negmax, u + 1)
                    act.wait_ge(on.scores_done, u + 1)
                    if u:
                        act.wait_ge(on.pt_psum, u)
                        act.wait_ge(on.pv_done, u - 1)
                    scale = 0.125 if kind == 1 else 1.0
                    for h in range(nh):
                        nc.scalar.activation(PR[:, h * nk:(h + 1) * nk, :], sc45[:, h * nk * P:(h + 1) * nk * P].rearrange("p (a b) -> p a b", b=P), ACT.Exp, scale=scale, bias=NM[:, u % 2, h:h + 1], accum_out=SU[:, u % 2, h:h + 1]).then_inc(on.probs if h == nh - 1 else on.probs_part, 1)
                    if kind == 1:
                        act.wait_ge(on.dsink, u + 1)
                        nc.scalar.activation(ES[:, u % 2, 0:nh], DS[:, u % 2, 0:nh], ACT.Exp).then_inc(on.esink, 1)
                elif k == "pt":
                    u = e[1]
                    act.wait_ge(on.pt_psum, u + 1)
                    if u:
                        act.wait_ge(on.pv_psum, u)
                    nc.scalar.activation(PT[:, 0:4], pt67[:, 0:512].rearrange("p (a b) -> p a b", b=P), ACT.Copy).then_inc(on.pt_part, 1)
                    nc.scalar.activation(PT[:, 4:8], pt67[:, 512:1024].rearrange("p (a b) -> p a b", b=P), ACT.Copy).then_inc(on.pt_done, 1)
                elif k == "yT":
                    u = e[1]
                    kind, n, h0, nh, nk = UNITS[u]
                    b0, nb = h0 // 2 + (4 if kind == 2 else 0), nh // 2
                    act.wait_ge(on.yT_psum, u + 1)
                    nc.scalar.activation(pyH[:, b0:b0 + nb, n * P:(n + 1) * P], ps[:, 4, 0:nb * P].rearrange("p (a b) -> p a b", b=P), ACT.Copy).then_inc(on.yTh, 1)
                elif k == "hprep":
                    s = e[1]
                    if e[2] == 0:
                        act.wait_ge(on.hdm, s + 1)
                        nc.scalar.activation(T2, T1, ACT.Exp).then_inc(on.hE1, 1)
                    elif e[2] == 1:
                        act.wait_ge(on.hE1, s + 1)
                        nc.scalar.activation(T1, T1, ACT.Exp, scale=-1.0).then_inc(on.hE2, 1)
                    elif e[2] == 2:
                        act.wait_ge(on.hQp, s + 1)
                        nc.scalar.activation(T2, hB, ACT.Exp).then_inc(on.hE3, 1)
                        nc.scalar.activation(E5[:], hB[:, :, C - 1:T:C], ACT.Exp).then_inc(on.hE5, 1)
                    else:
                        act.wait_ge(on.hdl, s + 1)
                        nc.scalar.activation(T1, T1, ACT.Exp).then_inc(on.hE4, 1)
                elif k == "hA":
                    s = e[1]
                    act.wait_ge(on.hkt_psum, s + 1)
                    for j in range(TB):
                        nc.scalar.activation(hKT[:, j], ps[:, 5 + j, :], ACT.Copy).then_inc(on.hkt, 1)
                elif k == "hC":
                    s = e[1]
                    for j in range(TB):
                        act.wait_ge(on.o_psum, 2 * s + j + 1)
                        v = ps[:, 4 + 3 * j, :].rearrange("p (h n) -> p h n", h=4)
                        nc.scalar.activation(T1[:, :, j * P:(j + 1) * P], v, ACT.Copy).then_inc(on.o_copy, 1)
                        nc.scalar.activation(T2[:, :, j * P:(j + 1) * P], v, ACT.Square).then_inc(on.o_sq, 1)
                elif k == "hD":
                    s = e[1]
                    act.wait_ge(on.oss_psum, s + 1)
                    nc.scalar.activation(oR0[:], ps[:, 5, 0:8], ACT.Sqrt, scale=1.0 / P,
                                         bias=eps[:, 0:1]).then_inc(on.o_rt, 1)
                elif k == "hsplit":
                    s = e[1]
                    act.wait_ge(on.hfin, s + 1)
                    act.wait_ge(*USED[PIDX["ba1", 1]])
                    nc.scalar.activation(pyH[:, 4 * s:4 * s + 4], YF0 if s == 0 else T1, ACT.Copy).then_inc(on.hsh, 1)
                elif k == "merge":
                    for kk in range(4 * e[1], 4 * e[1] + 4):
                        act.wait_ge(on.mixed, kk + 1)
                        nc.scalar.activation(p1H[:, kk], GA[:, kk], ACT.Copy).then_inc(on.mh, 1)
                elif k == "dt":
                    act.wait_ge(on.dt_abs, 1)
                    nc.scalar.activation(DE[:], DA[:], ACT.Exp).then_inc(on.dt_e, 1)
                    act.wait_ge(on.dt_e, 1)
                    nc.scalar.activation(DE[:], DE[:], ACT.Ln, bias=1.0).then_inc(on.dt_ln, 1)
                elif k == "sA":
                    act.wait_ge(on.seg, e[1] + 1)
                    nc.scalar.activation(SG, SG, ACT.Exp).then_inc(on.seg_exp, 1)
                elif k == "ysum":
                    nc.scalar.activation(fetch[:], eps[:], ACT.Sqrt).then_inc(on.act_fetch, 1)
                    for t in range(4):
                        act.wait_ge(on.yz, t + 1)
                        nc.scalar.activation(sT[:, t], sY[:, t], ACT.Square).then_inc(on.ysq, 1)
                    act.wait_ge(on.yss, 1)
                    nc.scalar.activation(R0[:], yss, ACT.Sqrt, scale=1.0 / 512, bias=eps[:, 0:1]).then_inc(on.yrt, 1)
                elif k == "snorm":
                    for t in range(4):
                        act.wait_ge(on.ytmp, t + 1)
                        nc.scalar.activation(pyH[:, t], sY[:, t], ACT.Copy).then_inc(on.snh, 1)
                elif k == "store":
                    for j in range(TB):
                        act.wait_ge(on.rd_done, 5)
                        act.wait_ge(on.ot_psum, j + 1)
                        nc.scalar.activation(OUT[:, j, 0:W], ps[:, 4 + 2 * j, :], ACT.Copy,
                                             scale=R1[:, j:j + 1]).then_inc(on.out_left, 1)

        @block.vector
        def _(dve):
            v = nc.vector

            steps = [0]

            def step(ins):
                steps[0] += 1
                ins.then_inc(on.dve_step, 1)
                dve.wait_ge(on.dve_step, steps[0])

            def tt(o, a, b, op):
                return v.tensor_tensor(o, a, b, op)

            def stt(o, a, s, b, op0, op1):
                return v.scalar_tensor_tensor(out=o, in0=a, scalar=s, in1=b, op0=op0, op1=op1)

            def split_lo(q):
                i = SIDX["w", q]
                nk = GROUPS[panels[q][0]]["parts"][panels[q][1]][1]
                wd = sum(w for _, w in GROUPS[panels[q][0]]["seg"])
                dve.wait_ge(on.w_hi, q + 1)
                tt(wL[:, q % NHL, 0:nk, 0:wd], raw[:, i % NRAW, 0:nk, 0:wd],
                       wH[:, q % NHL, 0:nk, 0:wd].bitcast(F32), ALU.subtract).then_inc(on.w_lo, 1)

            def norm(n):
                if n == 0:
                    dve.wait_ge(on.sq_done, KD)
                    v.reduce_sum(XSS[:], XS[:], AX_X).then_inc(on.ss_done, 1)
                if n == 2:
                    dve.wait_ge(on.ss_done, 3)
                    step(v.tensor_copy(S12[:], ps[:, 4:6, 0:2]))
                    stt(R2a[:], S12[:, :, 0], EPS, S12[:, :, 1], ALU.mult, ALU.add).then_inc(on.ms2_done, 1)
                    dve.wait_ge(on.rt2_done, 1)
                    v.reciprocal(R2a[:], R2a[:]).then_inc(on.rd2_done, 1)
                dve.wait_ge(on.rt_done, n + 1)
                v.reciprocal(R1[:], R0[:]).then_inc(on.rd_done, 1)
                src, gain = hT, {0: lambda k: pc("norm_mix_g", k), 1: lambda k: pc("norm_ffn_g", k),
                                 2: lambda k: am[:, k:k + 1],
                                 3: lambda k: af[:, k:k + 1]}.get(n)
                if n == 4:
                    return
                dve.wait_ge(on.bcast, n + 1)

                def low(k):
                    dve.wait_ge(on.uh_done, 8 * n + k + 1)
                    if n < 2:
                        tt(p1L[:, k], TMP[:, k], p1H[:, k].bitcast(F32), ALU.subtract).then_inc(on.u_ready, 1)
                    else:
                        o = (0 if n == 2 else 24) + k
                        stt(p1L[:, k], TMP[:, k], mod[:, o:o + 1], p1H[:, k].bitcast(F32), ALU.add,
                            ALU.subtract).then_inc(on.u_ready, 1)
                for k in range(KD):
                    stt(TMP[:, k], src[:, k], gain(k), rb, ALU.mult, ALU.mult).then_inc(on.tmp_done, 1)
                    if n and k == 1:
                        low(0)
                    elif k >= (3 if n else 2):
                        low(k - 2)
                    if n == 0 and k == 3:
                        split_lo(0)
                low(KD - 2)
                low(KD - 1)
                if n == 0:
                    split_lo(1)

            def evac(name):
                g = name.rstrip("0123456789")
                i = int(name[len(g):] or 0)
                if name in ("q0", "q1", "q2"):
                    return
                if name == "kv":
                    dve.wait_ge(on.evac_act, EV[name, 0][1])
                    dve.wait_ge(on.akz_zero, 1)
                    for gr in range(2):
                        for b in range(2):
                            v.tensor_copy(aKZ[C * b:C * b + C, 2 * gr + b], aK[C * gr:C * gr + C]).then_inc(on.kz, 1)
                            dve.wait_ge(on.kz, 2 * gr + b + 1)
                    dve.wait_ge(on.in_brow, 32)
                    for j in range(TB):
                        dve.wait_ge(on.tile_done, TILE[name, 1 + j])
                        tt(aV[:, j], ps[:, 2 + j, 0:P], vrow, ALU.add).then_inc(on.evac_dve, 1)
                elif g == "hq":
                    dve.wait_ge(on.evac_act, EV[name, 3][1])
                    tt(hQ, hQ, T1, ALU.mult).then_inc(on.hq_done, 1)
                elif g == "hf":
                    dve.wait_ge(on.lb_sig, 2)
                    for h in range(4):
                        dve.wait_ge(on.evac_act, EV[name, h][1])
                        v.tensor_scalar(hK[:, h], T2[:, h], oml[:, 4 * i + h:4 * i + h + 1], None,
                                        ALU.mult).then_inc(on.hk_done, 1)
                elif g == "hi":
                    if i:
                        dve.wait_ge(on.o_psum, 2 * i)
                    for j in range(TB):
                        dve.wait_ge(on.tile_done, TILE[name, j])
                        tt(hV[:, j], ps[:, 2 + j, :], brow[:, i * W:(i + 1) * W], ALU.add).then_inc(on.evac_dve, 1)
                elif g == "ba":
                    for m in range(4):
                        dve.wait_ge(on.tile_done, TILE[name, m])
                        tt(GA[:, 4 * i + m], ps[:, m, 0:T], GA[:, 4 * i + m], ALU.mult).then_inc(on.evac_dve, 1)
                elif g == "bh":
                    for m in range(4):
                        dve.wait_ge(on.tile_done, TILE[name, m])
                        tt(GB[:, 4 * i + m], ps[:, m, 0:T], GB[:, 4 * i + m], ALU.mult).then_inc(on.evac_dve, 1)
                        dve.wait_ge(on.evac_dve, EV[name, m][1])
                        tt(GA[:, 4 * i + m], GB[:, 4 * i + m], GA[:, 4 * i + m], ALU.add).then_inc(on.mixed, 1)
                elif g in ("out", "down"):
                    for m in range(4):
                        dve.wait_ge(on.tile_done, TILE[name, m])
                        tt(hT[:, 4 * i + m], ps[:, GROUPS[name]["tiles"][m][1], 0:T], hT[:, 4 * i + m], ALU.add).then_inc(on.evac_dve, 1)
                elif g in ("oo", "dd"):
                    for m in range(4):
                        o = (16 if g == "oo" else 40) + 4 * i + m
                        dve.wait_ge(on.tile_done, TILE[name, m])
                        stt(hT[:, 4 * i + m], ps[:, GROUPS[name]["tiles"][m][1], 0:T], mod[:, o:o + 1], hT[:, 4 * i + m], ALU.mult, ALU.add).then_inc(on.evac_dve, 1)
                        if name == "dd1" and m:
                            gained(4 + m - 1)
                    if name == "dd1":
                        gained(7)
                elif g == "f":
                    dve.wait_ge(on.z_ready, i)
                    for m in range(2):
                        dve.wait_ge(on.tile_done, TILE[name, 2 + m])
                        dve.wait_ge(on.evac_act, EV[name, m][1])
                        tt(ZT[:, m], ps[:, 2 + m, 0:T], TG[:, m], ALU.mult).then_inc(on.evac_dve, 1)
                elif name == "v2":
                    for j in range(TB):
                        dve.wait_ge(on.tile_done, TILE[name, j])
                        v.tensor_copy(v2[:, j], ps[:, 2 + j, :]).then_inc(on.evac_dve, 1)
                elif g in ("xs", "bc"):
                    s = int(g == "bc")
                    for tap in range(1, 4):
                        for m in range(4):
                            dve.wait_ge(on.conv0, 4 * s + m + 1)
                            dve.wait_ge(on.conv_done, 12 * s + max(4 * (tap - 2) + m + 1, 0))
                            stt(XC[:, 4 * s + m], XR[:, m, tap:tap + T], pc("conv_w", 8 * tap + 4 * s + m),
                                XC[:, 4 * s + m], ALU.mult, ALU.add).then_inc(on.conv_done, 1)
                elif g == "u":
                    for tap in range(1, 3):
                        for m in range(4):
                            wi = KF * 2 * tap + 2 * i + m % 2 + (KF if m > 1 else 0)
                            dve.wait_ge(on.uconv0, 4 * i + m + 1)
                            if tap == 2:
                                dve.wait_ge(on.uconv_done, 8 * i + m + 1)
                            stt(UC[:, m], UR[:, m, tap:tap + T], pc("ffn_conv_w", wi), UC[:, m], ALU.mult,
                                ALU.add).then_inc(on.uconv_done, 1)

            def tail(name):
                g = name.rstrip("0123456789")
                i = int(name[len(g):] or 0)
                if g == "hf":
                    for h in range(4):
                        dve.wait_ge(on.hf_log, 4 * i + h + 1)
                        v.tensor_tensor_scan(hB[:, h], reset[:], hB[:, h], 0.0, ALU.mult, ALU.add).then_inc(on.hb_done, 1)
                elif g == "f":
                    dve.wait_ge(on.zh_done, i + 1)
                    tt(zL[:, 2 * i:2 * i + 2], ZT, zH[:, 2 * i:2 * i + 2].bitcast(F32), ALU.subtract).then_inc(on.z_ready, 1)
                elif g == "u":
                    dve.wait_ge(on.uconv_done, 8 * i + 8)
                    dve.wait_ge(on.u_silu, i + 1)
                    dve.wait_ge(on.z_ready, NF + i)
                    tt(ZT, UC[:, 0:2], UC[:, 2:4], ALU.mult).then_inc(on.zt_done, 1)
                    dve.wait_ge(on.zt_done, i + 1)
                    dve.wait_ge(on.zh_done, NF + i + 1)
                    tt(zL[:, 2 * i:2 * i + 2], ZT, zH[:, 2 * i:2 * i + 2].bitcast(F32), ALU.subtract).then_inc(on.z_ready, 1)

            def gained(k):
                dve.wait_ge(*h_ready(4, k))
                v.tensor_scalar(OT[:, k], hT[:, k], pc("final_norm_w", k), None, ALU.mult).then_inc(on.ot_done, 1)

            dve.wait_ge(on.in_par, 16)
            tt(lbd[:], pc("lb0", 0, 8), pc("lb1", 0, 8), ALU.subtract).then_inc(on.lb_diff, 1)
            for e in TL:
                k = e[0]
                if k == "squares" and e[1] == 2:
                    v.memset(G12[:, :, 0], 1.0)
                    tt(G12[:, :, 1], pc("norm_final_g", 0, 8), pc("norm_final_g", 0, 8), ALU.mult).then_inc(on.gains2, 1)
                elif k == "load_x":
                    for b in range(4):
                        dve.wait_ge(on.x_psum, b + 1)
                        for kk in range(2):
                            v.tensor_copy(hT[:, 2 * b + kk], ps[:, 4 + b, kk * T:(kk + 1) * T]).then_inc(on.x_done, 1)
                elif k == "panel":
                    q = PIDX[e[1:]] + AHEAD
                    if q < len(panels):
                        split_lo(q)
                elif k == "norm":
                    norm(e[1])
                elif k == "evac":
                    evac(e[1])
                elif k == "tail":
                    tail(e[1])
                elif k == "gain":
                    for kk in range(4):
                        gained(kk)
                elif k == "store":
                    for j in range(TB):
                        dve.wait_ge(on.rd_done, 5)
                        dve.wait_ge(on.ot_psum, j + 1)
                        v.tensor_scalar(OUT[:, j, W:2 * W], ps[:, 5 + 2 * j, :], R1[:, j:j + 1], None,
                                        ALU.mult).then_inc(on.out_right, 1)
                elif k == "setup":
                    dve.wait_ge(on.a_exp, 1)
                    step(v.tensor_scalar(nega[:], nega[:], -1.0, None, ALU.mult))
                    v.tensor_scalar(negb[:], pc("b_in", 0, 58), -1.0, None, ALU.mult).then_inc(on.negb, 1)
                    dve.wait_ge(on.in_rel, 16)
                    step(v.memset(ext[:, 0:P - 1], 0.0))
                    v.tensor_scalar(ext[:, 0:P - 1], ext[:, 0:P - 1], ext[:, P - 1:P], None, ALU.add).then_inc(on.ext_done, 1)
                    dve.wait_ge(on.dtw_hi, 1)
                    tt(dtL[:], dtw, dtH[:].bitcast(F32), ALU.subtract).then_inc(on.dtw_lo, 1)
                elif k == "ada":
                    q = e[1]
                    i = SIDX["ada", q]
                    dve.wait_ge(on.raw[i % NRAW], landed[i])
                    if q % 2 == 0 and q:
                        dve.wait_ge(on.ada_psum, q // 2)
                    if q == 0:
                        dve.wait_ge(on.c_silu, 1)
                    for kk in range(KP):
                        c = cact[:, (q % 2) * KP + kk:(q % 2) * KP + kk + 1]
                        if kk == 0 and q % 2 == 0:
                            ins = v.tensor_scalar(acc[:], raw[:, i % NRAW, kk], c, None, ALU.mult)
                        else:
                            ins = stt(acc[:], raw[:, i % NRAW, kk], c, acc[:], ALU.mult, ALU.add)
                        if kk < KP - 1:
                            step(ins)
                    ins.then_inc(on.w_lo, 1)
                    dve.wait_ge(on.w_lo, i + 1)
                elif k == "ada_sum":
                    q = e[1]
                    dve.wait_ge(on.ada_psum, q + 1)
                    tt(mod[:, 4 * q:4 * q + 4], adaps, pc("b_ada", 4 * q, 4), ALU.add).then_inc(on.ada_done, 1)
                elif k == "mod":
                    dve.wait_ge(on.ada_done, 12)
                    step(stt(am[:], mod[:, 8:16], 1.0, pc("norm_mix_w_2", 0, 8), ALU.add, ALU.mult))
                    step(tt(am[:], am[:], pc("norm_final_g", 0, 8), ALU.mult))
                    step(stt(af[:], mod[:, 32:40], 1.0, pc("norm_ffn_w_2", 0, 8), ALU.add, ALU.mult))
                elif k == "scores":
                    u = e[1]
                    kind, n, h0, nh, nk = UNITS[u]
                    pu = u % 2
                    dve.wait_ge(on.scores_done, u + 1)
                    if u > 1:
                        dve.wait_ge(on.probs, u - 1)
                    step(v.reduce_max(RM[:, pu, 0:nh], sc45[:, 0:nh * nk * P].rearrange("p (h k) -> p h k", h=nh), AX_X))
                    if kind == 1:
                        step(stt(RM[:, pu, 0:nh], RM[:, pu, 0:nh], 0.125, pc("sinks", h0, nh), ALU.mult, ALU.max))
                    v.tensor_scalar(NM[:, pu, 0:nh], RM[:, pu, 0:nh], -1.0, None, ALU.mult).then_inc(on.negmax, 1)
                    dve.wait_ge(on.negmax, u + 1)
                    if kind == 1:
                        tt(DS[:, pu, 0:nh], NM[:, pu, 0:nh], pc("sinks", h0, nh), ALU.add).then_inc(on.dsink, 1)
                        dve.wait_ge(on.dsink, u + 1)
                elif k == "pv":
                    u = e[1]
                    kind, n, h0, nh, nk = UNITS[u]
                    dve.wait_ge(on.probs, u + 1)
                    if kind == 1:
                        dve.wait_ge(on.esink, u + 1)
                        step(tt(SU[:, u % 2, 0:nh], SU[:, u % 2, 0:nh], ES[:, u % 2, 0:nh], ALU.add))
                    step(v.reciprocal(RD[:, u % 2, 0:nh], SU[:, u % 2, 0:nh]))
                    dve.wait_ge(on.pv_psum, u + 1)
                    if u:
                        dve.wait_ge(on.yT_psum, u)
                    tt(YT[:, 0:nh * DH].rearrange("p (h d) -> p h d", h=nh),
                           ps[:, 6, 0:nh * DH].rearrange("p (h d) -> p h d", h=nh),
                           RD[:, u % 2, 0:nh].unsqueeze(2).broadcast_to([P, nh, DH]), ALU.mult).then_inc(on.pv_done, 1)
                elif k == "yT":
                    u = e[1]
                    kind, n, h0, nh, nk = UNITS[u]
                    b0, nb = h0 // 2 + (4 if kind == 2 else 0), nh // 2
                    dve.wait_ge(on.yTh, u + 1)
                    tt(pyL[:, b0:b0 + nb, n * P:(n + 1) * P],
                           ps[:, 4, 0:nb * P].rearrange("p (a b) -> p a b", b=P),
                           pyH[:, b0:b0 + nb, n * P:(n + 1) * P].bitcast(F32), ALU.subtract).then_inc(on.yT_done, 1)
                elif k == "hprep":
                    s = e[1]
                    bc = hB.rearrange("p h n -> p (h n)").rearrange("p (c n) -> p c n", n=C)
                    f = lambda t: t.rearrange("p h n -> p (h n)").rearrange("p (c n) -> p c n", n=C)
                    if e[2] == 0:
                        dve.wait_ge(on.hb_done, 4 * s + 4)
                        dve.wait_ge(on.hk_done, 4 * s + 4)
                        tt(f(T1), bc, bc[:, :, C // 2 - 1:C // 2].broadcast_to([P, 16, C]), ALU.subtract).then_inc(on.hdm, 1)
                    elif e[2] == 1:
                        if s == 0:
                            dve.wait_ge(on.scores_done, NU1)
                        dve.wait_ge(on.hE1, s + 1)
                        tt(hQp, hQ, T2, ALU.mult).then_inc(on.hQp, 1)
                        dve.wait_ge(on.hE2, s + 1)
                        tt(hKp, hK, T1, ALU.mult).then_inc(on.hKp, 1)
                    elif e[2] == 2:
                        dve.wait_ge(on.hKp, s + 1)
                        tt(f(T1), bc[:, :, C - 1:C].broadcast_to([P, 16, C]), bc, ALU.subtract).then_inc(on.hdl, 1)
                    else:
                        dve.wait_ge(on.hE4, s + 1)
                        tt(hK, hK, T1, ALU.mult).then_inc(on.hKk, 1)
                elif k == "hA":
                    s = e[1]
                    dve.wait_ge(on.hat_zero, s + 1)
                    dve.wait_ge(on.hat_psum, s + 1)
                    for c in range(2):
                        r = slice(C * c, C * c + C)
                        v.copy_predicated(hAT[r, :, r], hmask[r, :].unsqueeze(1).broadcast_to([C, 8, C]),
                                              ps[r, 4, :].rearrange("p (a b) -> p a b", b=C)).then_inc(on.hat, 1)
                elif k == "hB":
                    s = e[1]
                    bank = (7, 5, 6)
                    dve.wait_ge(on.hE5, s + 1)
                    dve.wait_ge(on.hkv_psum, 3 * s + 1)
                    v.tensor_copy(hS[:, 0], ps[:, 7, :]).then_inc(on.hS, 1)
                    dve.wait_ge(on.hS, 9 * s + 1)
                    for c in (1, 2):
                        dve.wait_ge(on.hkv_psum, 3 * s + c + 1)
                        for h in range(4):
                            cs = slice(h * P, h * P + P)
                            ins = stt(hS[:, c, cs], hS[:, c - 1, cs], E5[:, h, c:c + 1], ps[:, bank[c], cs], ALU.mult,
                                      ALU.add)
                            ins.then_inc(on.hS, 1)
                        dve.wait_ge(on.hS, 9 * s + 4 * c + 1)
                elif k == "hD":
                    s = e[1]
                    dve.wait_ge(on.o_rt, s + 1)
                    v.reciprocal(oR1[:], oR0[:]).then_inc(on.o_rd, 1)
                    dve.wait_ge(on.o_bcast, s + 1)
                    step(tt(T1.rearrange("p h n -> p (h n)").rearrange("p (b n) -> p b n", b=2),
                            T1.rearrange("p h n -> p (h n)").rearrange("p (b n) -> p b n", b=2), ps[:, 5:7, :], ALU.mult))
                    for h in range(4):
                        ins = stt((YF0 if s == 0 else T1)[:, h], T1[:, h], pc("hgrn_norm_g", 4 * s + h), hG[:, h],
                                  ALU.mult, ALU.mult)
                        if h < 3:
                            step(ins)
                    ins.then_inc(on.hfin, 1)
                    dve.wait_ge(on.hfin, s + 1)
                elif k == "hsplit":
                    s = e[1]
                    dve.wait_ge(on.hsh, s + 1)
                    tt(pyL[:, 4 * s:4 * s + 4], YF0 if s == 0 else T1, pyH[:, 4 * s:4 * s + 4].bitcast(F32),
                           ALU.subtract).then_inc(on.hs_done, 1)
                elif k == "merge":
                    for kk in range(4 * e[1], 4 * e[1] + 4):
                        dve.wait_ge(on.mh, kk + 1)
                        tt(p1L[:, kk], GA[:, kk], p1H[:, kk].bitcast(F32), ALU.subtract).then_inc(on.merged, 1)
                elif k == "h_final":
                    for kk in range(KD):
                        if kk == 0:
                            dve.wait_ge(on.bcast2, 1)
                        stt(hT[:, kk], hT[:, kk], pc("norm_final_g", kk), rb2, ALU.mult,
                            ALU.mult).then_inc(on.h_final, 1)
                elif k == "dt":
                    dve.wait_ge(on.dt_psum, 1)
                    f = lambda n: pc(n, 0, 8).unsqueeze(1).broadcast_to([P, TB, 8])
                    step(tt(DT[:], ps[:, 7, 0:16].rearrange("p (j h) -> p j h", j=TB), f("dt_bias"), ALU.add))
                    step(v.tensor_scalar(DR[:], DT[:], -1.0, None, ALU.mult))
                    tt(DA[:], DT[:], DR[:], ALU.min).then_inc(on.dt_abs, 1)
                    dve.wait_ge(on.dt_abs, 1)
                    step(v.tensor_scalar(DR[:], DT[:], 0.0, None, ALU.max))
                    dve.wait_ge(on.dt_ln, 1)
                    step(tt(DT[:], DR[:], DE[:], ALU.add))
                    tt(ADT[:], DT[:], nega[:].unsqueeze(1).broadcast_to([P, TB, 8]), ALU.mult).then_inc(on.adt, 1)
                    dve.wait_ge(on.adt, 1)
                elif k == "xdt":
                    for j in range(TB):
                        dve.wait_ge(on.xd_psum, j + 1)
                        tt(XD[:, j].rearrange("p (h d) -> p h d", h=8),
                               ps[:, 6 + j, :].rearrange("p (h d) -> p h d", h=8),
                               DT[:, j].unsqueeze(2).broadcast_to([P, 8, DH]), ALU.mult).then_inc(on.xd, 1)
                elif k == "sA":
                    g = e[1]
                    if g == 0:
                        dve.wait_ge(on.bm_psum, 1)
                        step(v.tensor_copy(Bs[:], ps[:, 7, 64:112].rearrange("p (a b) -> p a b", b=8)))
                    dve.wait_ge(on.abc_psum, g + 1)
                    if g:
                        dve.wait_ge(on.sy_psum, g)
                    for x in range(6):
                        c = x if x < 4 else x - 2
                        step(tt(SG[:, :, x * C:(x + 1) * C],
                                sc45.rearrange("p (h n) -> p h n", h=4)[:, :, c * C:(c + 1) * C],
                                Bs[:, x, 4 * g:4 * g + 4].unsqueeze(2).broadcast_to([P, 4, C]), ALU.add))
                    v.tensor_scalar(SG, SG, 0.0, None, ALU.min).then_inc(on.seg, 1)
                    dve.wait_ge(on.seg, g + 1)
                    dve.wait_ge(on.cb_psum, g + 1)
                    step(tt(CB[:, 0:P], ps[:, 6, 0:P], UT[:], ALU.mult))
                    step(v.tensor_copy(CB[:, P:T], ps[:, 6, P:T]))
                    tt(CB[:, T:T + P], ps[:, 6, T:T + P], UT[:], ALU.mult).then_inc(on.cb, 1)
                    dve.wait_ge(on.cb, g + 1)
                    dve.wait_ge(on.seg_exp, g + 1)
                    tt(SG, SG, CB.unsqueeze(1).broadcast_to([P, 4, 384]), ALU.mult).then_inc(on.g_done, 1)
                    dve.wait_ge(on.g_done, g + 1)
                elif k == "sY":
                    g = e[1]
                    dve.wait_ge(on.sy_psum, g + 1)
                    for t in range(2):
                        stt(sY[:, 2 * g + t], XC[:, 2 * g + t], pc("d_skip", 2 * g + t),
                                 ps[:, 7, t * T:(t + 1) * T], ALU.mult, ALU.add).then_inc(on.sy, 1)
                        dve.wait_ge(on.sy, 2 * g + t + 1)
                elif k == "ysum":
                    for t in range(4):
                        dve.wait_ge(*EV["z", t])
                        tt(sY[:, t], sY[:, t], sZ[:, t], ALU.mult).then_inc(on.yz, 1)
                    dve.wait_ge(on.yrt, 1)
                    v.reciprocal(R1[:], R0[:]).then_inc(on.yrd, 1)
                elif k == "snorm":
                    dve.wait_ge(on.yz, 4)
                    dve.wait_ge(on.ybcast, 1)

                    def low(t):
                        dve.wait_ge(on.snh, t + 1)
                        tt(pyL[:, t], sY[:, t], pyH[:, t].bitcast(F32), ALU.subtract).then_inc(on.snorm_done, 1)
                    for t in range(4):
                        stt(sY[:, t], sY[:, t], pc("ssd_norm_w", t), yrb, ALU.mult, ALU.mult).then_inc(on.ytmp, 1)
                        if t >= 2:
                            low(t - 2)
                    low(2)
                    low(3)
                if k == "norm" and e[1] == 2:
                    v.memset(XR[:, :, 0:3], 0.0).then_inc(on.xr_zero, 1)
                if k == "norm" and e[1] == 3:
                    v.memset(UR[:, :, 0:2], 0.0).then_inc(on.ur_zero, 1)

        @block.tensor
        def _(pe):
            mm = nc.tensor.matmul

            def tr(o, i):
                return nc.tensor.transpose(o, i, ident[:])

            def spread(o, column):
                return mm(o, column.broadcast_to([P, P]), ident[:], start=True, stop=True)

            def two_sums(k):
                pe.wait_ge(on.sq_done, 16 + k + 1)
                for j in range(TB):
                    last = mm(ps[:, 4 + j, 0:2], SQ[:, k, j * P:(j + 1) * P], G12[:, k], start=k == 0, stop=k == KD - 1)
                return last

            def turn(k):
                pe.wait_ge(on.ot_done, k + 1)
                for j in range(TB):
                    last = tr(ps[:, 4 + 2 * j + k // 4, (k % 4) * P:(k % 4 + 1) * P], OT[:, k, j * P:(j + 1) * P])
                    if k == KD - 1:
                        last.then_inc(on.ot_psum, 1)

            ada_sums = [0]

            def panel(name, part):
                q = PIDX[name, part]
                g = GROUPS[name]
                k0, nk = g["parts"][part]
                aH, aL = OPND[g["act"]]
                slot = q % NHL
                final = part == len(g["parts"]) - 1
                pe.wait_ge(on.w_lo, SIDX["w", q] + 1)

                def product(t, k):
                    for x, (wt, at_) in enumerate(((wH, aH), (wH, aL), (wL, aH))):
                        st = part == 0 and k == 0 and x == 0
                        en = final and k == nk - 1 and x == 2
                        if t[0] == "cm":
                            last = mm(ps[:, t[1], 0:T], wt[:, slot, k, t[2]:t[2] + P], at_[:, k0 + k, :],
                                      start=st, stop=en)
                        else:
                            last = mm(ps[:, t[1], 0:t[3]], at_[:, k0 + k, t[4] * P:(t[4] + 1) * P],
                                      wt[:, slot, k, t[2]:t[2] + t[3]], start=st, stop=en)
                    return last

                if part == 0 and name in FIRST_USE:
                    for m, t in enumerate(g["tiles"]):
                        if (name, m) in BANKFREE:
                            pe.wait_ge(*BANKFREE[name, m])
                    for k in range(nk):
                        pe.wait_ge(*operand_ready(name, k))
                        for t in g["tiles"]:
                            last = product(t, k)
                else:
                    for m, t in enumerate(g["tiles"]):
                        if part == 0 and (name, m) in BANKFREE:
                            pe.wait_ge(*BANKFREE[name, m])
                        for k in range(nk):
                            if m == 0 and name in FIRST_USE:
                                pe.wait_ge(*operand_ready(name, k0 + k))
                            last = product(t, k)
                        if final:
                            last.then_inc(on.tile_done, 1)
                if not final:
                    last.then_inc(on.panel_done, 1)

            pe.wait_ge(on.pool_step, 6)
            for e in TL:
                k = e[0]
                if k == "load_x":
                    for b in range(4):
                        pe.wait_ge(on.in_x[b], 16)
                        for kk in range(2):
                            for j in range(TB):
                                last = tr(ps[:, 4 + b, kk * T + j * P:kk * T + (j + 1) * P],
                                          xtok[:, j, (2 * b + kk) * P:(2 * b + kk + 1) * P])
                        last.then_inc(on.x_psum, 1)
                elif k == "panel":
                    panel(e[1], e[2])
                elif k == "norm":
                    n = e[1]
                    pe.wait_ge(on.ada_done, ada_sums[0])
                    if n == 0:
                        pe.wait_ge(on.x_done, KD)
                    if n == 4:
                        for kk in range(4, KD - 1):
                            turn(kk)
                        pe.wait_ge(*EV["dd1", 1])
                    sums = ssf if n == 4 else ss
                    if n == 2:
                        for kk in range(4, KD):
                            last = two_sums(kk)
                    for kk in (0, 4, 5, 6, 7) if n in (1, 3, 4) else ():
                        if kk:
                            pe.wait_ge(on.sq_done, 8 * n + kk + 1)
                        else:
                            pe.wait_ge(on.sq_sum, {1: 1, 3: 2, 4: 3}[n])
                        for j in range(TB):
                            last = mm(sums[:, j:j + 1], SQ[:, kk, j * P:(j + 1) * P], ones[:, 0:1], start=kk == 0,
                                      stop=kk == KD - 1)
                    if n:
                        last.then_inc(on.ss_done, 1)
                    if n == 4:
                        turn(KD - 1)
                        continue
                    if n == 2:
                        pe.wait_ge(on.rd2_done, 1)
                        for j in range(TB):
                            last = spread(rb[:, j * P:(j + 1) * P], R2a[:, j:j + 1])
                        last.then_inc(on.bcast, 1)
                        pe.wait_ge(on.rd_done, n + 1)
                        for j in range(TB):
                            last = spread(rb2[:, j * P:(j + 1) * P], R1[:, j:j + 1])
                        last.then_inc(on.bcast2, 1)
                    else:
                        pe.wait_ge(on.rd_done, n + 1)
                        for j in range(TB):
                            last = spread(rb[:, j * P:(j + 1) * P], R1[:, j:j + 1])
                        last.then_inc(on.bcast, 1)
                elif k == "first_sums":
                    pe.wait_ge(on.gains2, 1)
                    for kk in range(4):
                        two_sums(kk)
                elif k == "ada_sum":
                    q = e[1]
                    pe.wait_ge(on.w_lo, SIDX["ada", 2 * q + 1] + 1)
                    pe.wait_ge(on.ada_done, q)
                    if q == 0:
                        pe.wait_ge(on.x_done, KD)
                    elif q == 2:
                        pe.wait_ge(on.o_sq, 4)
                    elif q == 7:
                        pe.wait_ge(on.tmp_done, 16)
                    for t in range(4):
                        last = mm(adaps[:, t:t + 1], acc[:, t * P:(t + 1) * P], ones[:, 0:1], start=True, stop=True)
                    last.then_inc(on.ada_psum, 1)
                    ada_sums[0] += 1
                elif k == "scores":
                    u = e[1]
                    kind, n, h0, nh, nk = UNITS[u]
                    if u:
                        pe.wait_ge(on.probs, u)
                    if u > 1:
                        pe.wait_ge(on.yT_done, u - 1)
                    if kind == 1:
                        pe.wait_ge(on.consts, 1)
                        pe.wait_ge(*EV["q1", 3])
                        pe.wait_ge(on.kz, 4)
                        pe.wait_ge(on.ada_done, ada_sums[0])
                    else:
                        pe.wait_ge(*EV["q2", 3])
                        pe.wait_ge(*EV["k2", 3])
                        pe.wait_ge(on.in_R2, 16)
                        pe.wait_ge(on.seg, 2)
                    for hh in range(nh):
                        h = h0 + hh
                        o = sc45[:, hh * nk * P:(hh + 1) * nk * P]
                        ks = slice(0, nk * P) if n else slice(0, P)
                        if kind == 1:
                            mm(o, identb[:], mask1[:, (2 - nk) * P:2 * P], start=True, stop=False)
                            last = mm(o, aQ[:, h // 2, n * P:(n + 1) * P], aKZ[:, 2 * (h // 8) + h % 2, ks],
                                      start=False, stop=True)
                        else:
                            mm(o, J[:], R2[:, h, (2 - nk) * P:2 * P], start=True, stop=False)
                            mm(o[:, (nk - 1) * P:nk * P], identb[:], mask2[:], start=False, stop=False)
                            last = mm(o, q2[:, h // 2, n * P:(n + 1) * P], k2z[:, h, ks], start=False, stop=True)
                    last.then_inc(on.scores_done, 1)
                elif k == "pt":
                    u = e[1]
                    pe.wait_ge(on.probs, u + 1)
                    if u:
                        pe.wait_ge(on.pv_done, u)
                        pe.wait_ge(on.pt_done, u)
                    if u == NU1:
                        pe.wait_ge(on.sy, 4)
                        pe.wait_ge(on.cb, 2)
                    if u == len(UNITS) - 1:
                        pe.wait_ge(on.ytmp, 4)
                    for b in range(8):
                        last = tr(pt67[:, b * P:(b + 1) * P], PR[:, b, :])
                    last.then_inc(on.pt_psum, 1)
                elif k == "pv":
                    u = e[1]
                    kind, n, h0, nh, nk = UNITS[u]
                    pe.wait_ge(on.pt_done, u + 1)
                    if kind == 1:
                        pe.wait_ge(*EV["kv", 2])
                    else:
                        pe.wait_ge(*EV["v2", 1])
                    for hh in range(nh):
                        h = h0 + hh
                        for kb in range(nk):
                            vv = aV[:, kb, (h // 8) * DH:(h // 8 + 1) * DH] if kind == 1 else v2[:, kb, h * DH:(h + 1) * DH]
                            last = mm(ps[:, 6, hh * DH:(hh + 1) * DH], PT[:, hh * nk + kb, :], vv, start=kb == 0,
                                      stop=kb == nk - 1)
                    last.then_inc(on.pv_psum, 1)
                elif k == "yT":
                    u = e[1]
                    kind, n, h0, nh, nk = UNITS[u]
                    pe.wait_ge(on.pv_done, u + 1)
                    nxt = u + 1 < len(UNITS) and UNITS[u + 1][0] == kind
                    pe.wait_ge(on.probs, u + 1 + nxt)
                    for b in range(nh // 2):
                        last = tr(ps[:, 4, b * P:(b + 1) * P], YT[:, b * P:(b + 1) * P])
                    last.then_inc(on.yT_psum, 1)
                elif k == "hA":
                    s = e[1]
                    pe.wait_ge(on.hKp, s + 1)
                    pe.wait_ge(on.hKk, s + 1)
                    if s == 0:
                        pe.wait_ge(on.yT_done, NU1)
                        pe.wait_ge(on.pv_done, NU1)
                        pe.wait_ge(on.probs, NU1)
                    else:
                        pe.wait_ge(on.o_sq, 2 * s)
                        pe.wait_ge(on.o_rt, s)
                    for j in range(TB):
                        for h in range(4):
                            for c in range(2):
                                t0 = j * P + c * C
                                last = mm(ps[C * c:C * c + C, 4, (4 * j + h) * C:(4 * j + h + 1) * C],
                                          hKp[:, h, t0:t0 + C], hQp[:, h, t0:t0 + C], start=True, stop=True)
                    last.then_inc(on.hat_psum, 1)
                    for j in range(TB):
                        for h in range(4):
                            last = tr(ps[:, 5 + j, h * P:(h + 1) * P], hK[:, h, j * P:(j + 1) * P])
                    last.then_inc(on.hkt_psum, 1)
                elif k == "hB":
                    s = e[1]
                    pe.wait_ge(*EV[f"hi{s}", 1])
                    pe.wait_ge(on.hkt, 2 * s + 2)
                    for c in range(3):
                        r = slice(C * (c % 2), C * (c % 2) + C)
                        for h in range(4):
                            cs = slice(h * P, h * P + P)
                            last = mm(ps[:, (7, 5, 6)[c], cs], hKT[r, c // 2, cs], hV[r, c // 2, cs], start=True,
                                      stop=True)
                        last.then_inc(on.hkv_psum, 1)
                elif k == "hC":
                    s = e[1]
                    pe.wait_ge(on.hat, 2 * s + 2)
                    pe.wait_ge(on.hS, 9 * s + 9)
                    pe.wait_ge(on.hQq, s + 1)
                    for j in range(TB):
                        for h in range(4):
                            o = ps[:, 4 + 3 * j, h * P:(h + 1) * P]
                            cs = slice(h * P, h * P + P)
                            mm(o, hV[:, j, cs], hAT[:, 4 * j + h, :], start=True, stop=False)
                            for c in range(2):
                                if 2 * j + c:
                                    last = mm(o[:, c * C:(c + 1) * C], hS[:, 2 * j + c - 1, cs],
                                              hQ[:, h, j * P + c * C:j * P + (c + 1) * C], start=False, stop=c == 1)
                        last.then_inc(on.o_psum, 1)
                elif k == "hD":
                    s = e[1]
                    pe.wait_ge(on.o_sq, 2 * s + 2)
                    for h in range(4):
                        for j in range(TB):
                            last = mm(ps[:, 5, 2 * h + j:2 * h + j + 1], T2[:, h, j * P:(j + 1) * P], ones[:, 0:1],
                                      start=True, stop=True)
                    last.then_inc(on.oss_psum, 1)
                    pe.wait_ge(on.o_rd, s + 1)
                    for x in range(8):
                        last = spread(ps[:, 5 + x // 4, (x % 4) * P:(x % 4 + 1) * P], oR1[:, x:x + 1])
                    last.then_inc(on.o_bcast, 1)
                elif k == "dt":
                    pe.wait_ge(on.dtw_lo, 1)
                    pe.wait_ge(on.h_final, KD)
                    for j in range(TB):
                        for kk in range(KD):
                            pe.wait_ge(on.u_ready, 16 + kk + 1)
                            js = slice(j * P, (j + 1) * P)
                            for x, (wt, at_) in enumerate(((dtH, p1H), (dtH, p1L), (dtL, p1H))):
                                last = mm(ps[:, 7, j * 8:(j + 1) * 8], at_[:, kk, js], wt[:, kk, :],
                                          start=kk == 0 and x == 0, stop=kk == KD - 1 and x == 2)
                    last.then_inc(on.dt_psum, 1)
                elif k == "xdt":
                    pe.wait_ge(on.xc_done, 1)
                    pe.wait_ge(on.adt, 1)
                    for j in range(TB):
                        for t in range(4):
                            last = tr(ps[:, 6 + j, t * P:(t + 1) * P], XC[:, t, j * P:(j + 1) * P])
                        last.then_inc(on.xd_psum, 1)
                elif k == "sA":
                    g = e[1]
                    pe.wait_ge(on.adt, 1)
                    if g:
                        pe.wait_ge(on.seg, g)
                        pe.wait_ge(on.cb, g)
                    a = sc45.rearrange("p (h n) -> p h n", h=4)
                    for h in range(4):
                        for j in range(TB):
                            last = mm(a[:, h, j * P:(j + 1) * P], ADT[:, j, 4 * g + h:4 * g + h + 1].broadcast_to([P, P]),
                                      CL[:], start=True, stop=True)
                    last.then_inc(on.abc_psum, 1)
                    pe.wait_ge(on.xd, 2)
                    if g == 0:
                        for x, terms in enumerate((((M0, 0),), ((M1, 0),), ((SL, 0),), ((SL, 0), (OL, 1)),
                                                   ((M0, 1),), ((M1, 1),))):
                            for y, (mat, j) in enumerate(terms):
                                last = mm(ps[:, 7, 64 + 8 * x:72 + 8 * x], mat[:], ADT[:, j, :], start=y == 0,
                                          stop=y == len(terms) - 1)
                        last.then_inc(on.bm_psum, 1)
                    pe.wait_ge(on.xc_done, 2)
                    mm(ps[:, 6, 0:T], XC[:, 4 + g, 0:P], XC[:, 6 + g, :], start=True, stop=True)
                    last = mm(ps[:, 6, T:T + P], XC[:, 4 + g, P:T], XC[:, 6 + g, P:T], start=True, stop=True)
                    last.then_inc(on.cb_psum, 1)
                elif k == "sY":
                    g = e[1]
                    pe.wait_ge(on.g_done, g + 1)
                    if g:
                        pe.wait_ge(on.sy, 2 * g)
                    for hh in range(4):
                        h = 4 * g + hh
                        o = ps[C * (hh % 2):C * (hh % 2) + C, 7, (hh // 2) * T:(hh // 2 + 1) * T]
                        mm(o, XD[:, 0, h * DH:(h + 1) * DH], SG[:, hh, 0:T], start=True, stop=False)
                        last = mm(o[:, P:T], XD[:, 1, h * DH:(h + 1) * DH], SG[:, hh, T:T + P], start=False, stop=True)
                    last.then_inc(on.sy_psum, 1)
                elif k == "ysum":
                    pe.wait_ge(on.pv_done, 8)
                    pe.wait_ge(on.pt_done, 8)
                    for t in range(4):
                        pe.wait_ge(on.ysq, t + 1)
                        for j in range(TB):
                            last = mm(yss[:, j:j + 1], sT[:, t, j * P:(j + 1) * P], ones[:, 0:1], start=t == 0,
                                      stop=t == 3)
                    last.then_inc(on.yss, 1)
                elif k == "snorm":
                    pe.wait_ge(on.yrd, 1)
                    for j in range(TB):
                        last = spread(yrb[:, j * P:(j + 1) * P], R1[:, j:j + 1])
                    last.then_inc(on.ybcast, 1)
                elif k == "turn":
                    for kk in range(4):
                        turn(kk)


INPUTS = ["x", "w_in", "b_in", "w_branch_attn", "w_branch_hgrn", "w_out", "w_ffn_gate", "w_ffn_up", "w_ffn_down",
          "w_ada_2", "w_in_2", "w_out_2", "w_up_2", "w_down_2"]


def kernel(**inputs):
    import numpy as np
    import concourse.bacc as bacc
    from concourse.bass_utils import run_bass_kernel_spmd

    def cols(a):
        return np.asarray(a).reshape(-1, P).T

    def rows(a):
        return np.broadcast_to(np.asarray(a).reshape(1, -1), (P, np.asarray(a).size))

    lb = np.asarray(inputs["hgrn_lb_logits"])
    params = np.concatenate([
        cols(inputs["norm_mix_g"]), cols(inputs["b_in"]), cols(lb[0]), cols(lb[1]), cols(inputs["hgrn_norm_g"]),
        cols(inputs["norm_ffn_g"]), cols(inputs["norm_final_g"]), cols(inputs["c_2"]), cols(inputs["norm_mix_w_2"]),
        cols(inputs["b_ada_2"]), cols(inputs["ssd_conv_w_2"]), cols(inputs["ssd_conv_b_2"]),
        cols(np.repeat(np.asarray(inputs["d_skip_2"]).reshape(-1), 64)), cols(inputs["ssd_norm_w_2"]),
        cols(inputs["norm_ffn_w_2"]), cols(inputs["ffn_conv_w_2"]), cols(inputs["final_norm_w_2"]),
        rows(inputs["attn_sinks"]), rows(inputs["dt_bias_2"]), rows(inputs["a_log_2"])], axis=1)
    nc = bacc.Bacc("TRN2", target_bir_lowering=False, num_devices=1)
    given = {name: np.ascontiguousarray(inputs[name]) for name in INPUTS}
    given["params"] = np.ascontiguousarray(params)
    given["rel_rev"] = np.ascontiguousarray(np.asarray(inputs["rel_bias_2"])[0, :, ::-1])
    arrays, IN = {}, {}
    for name, a in given.items():
        arrays["in_" + name] = a
        IN[name] = nc.dram_tensor("in_" + name, a.shape, mybir.dt.from_np(a.dtype), kind="ExternalInput").ap()
    out = nc.dram_tensor("out", (1, T, D), F32, kind="ExternalOutput").ap()
    build(nc, IN, out)
    return run_bass_kernel_spmd(nc, [arrays], core_ids=[0]).results[0]["out"]
```
